# Optimizing a Trainium2 kernel written in Bass

```python
import numpy as np
import jax, jax.numpy as jnp
from jax import lax
import math

D_MODEL = 1024
BATCH = 1
SEQ = 256
DEPTH = 1

D_CONV = D_MODEL
CONV_WIDTH = 3
HEAD_DIM = 64
HEADS_PER_GROUP = 8
DILATED_GROUPS = ((128, 1), (512, 4), (2048, 16))
N_ATTN_HEADS = HEADS_PER_GROUP * len(DILATED_GROUPS)
D_ATTN = N_ATTN_HEADS * HEAD_DIM
D_ATTN_OUT = HEADS_PER_GROUP * HEAD_DIM
BLOCK = 128
ROT_DIM = HEAD_DIM // 4
ROPE_THETA = 500000.0
PEER_HEADS = 8
PEER_N_KEYS = 128
PEER_N_EXPERTS = PEER_N_KEYS * PEER_N_KEYS
PEER_TOPK = 16
PEER_D_HALF = 128
PEER_D_QUERY = 2 * PEER_D_HALF
PEER_CHUNK = 128
RMS_EPS = 1e-6


def rms_norm(x, g):
    xf = x.astype(jnp.float32)
    y = xf * lax.rsqrt(jnp.mean(xf * xf, axis=-1, keepdims=True) + RMS_EPS)
    return (y * g.astype(jnp.float32)).astype(x.dtype)

def partial_rotary(t, positions):
    half = ROT_DIM // 2
    inv_freq = ROPE_THETA ** (-jnp.arange(half, dtype=jnp.float32) * (2.0 / ROT_DIM))
    ang = positions.astype(jnp.float32)[..., None] * inv_freq
    cos = jnp.cos(ang)[:, :, None, :]
    sin = jnp.sin(ang)[:, :, None, :]
    tr = t[..., :ROT_DIM].astype(jnp.float32)
    t1, t2 = tr[..., :half], tr[..., half:]
    rot = jnp.concatenate([t1 * cos - t2 * sin, t2 * cos + t1 * sin], axis=-1).astype(t.dtype)
    return jnp.concatenate([rot, t[..., ROT_DIM:]], axis=-1)

def dilated_window_attention(q, k, v, window, dilation):
    B, S, H, Dh = q.shape
    steps = window // dilation
    span = dilation * BLOCK
    sp = -(-S // span) * span
    nb = sp // span

    def blocks(t):
        t = jnp.pad(t, ((0, 0), (0, sp - S), (0, 0), (0, 0)))
        return t.reshape(B, nb, BLOCK, dilation, H, Dh)

    def with_prev(t):
        prev = jnp.pad(t, ((0, 0), (1, 0), (0, 0), (0, 0), (0, 0), (0, 0)))[:, :-1]
        return jnp.concatenate([prev, t], axis=2)

    qb = blocks(q)
    kk = with_prev(blocks(k))
    vv = with_prev(blocks(v))
    s = jnp.einsum('bnqrhd,bnkrhd->bnrhqk', qb, kk,
                   preferred_element_type=jnp.float32) * (Dh ** -0.5)
    qi = np.arange(BLOCK)[:, None]
    ki = np.arange(2 * BLOCK)[None, :]
    dist = BLOCK + qi - ki
    band = (dist >= 0) & (dist <= steps)
    valid = band[None] & ((np.arange(nb)[:, None, None] > 0) | (ki >= BLOCK)[None])
    s = jnp.where(valid[None, :, None, None], s, -jnp.inf)
    m = jnp.max(s, axis=-1, keepdims=True)
    p = jnp.exp(s - m)
    l = jnp.sum(p, axis=-1, keepdims=True)
    o = jnp.einsum('bnrhqk,bnkrhd->bnqrhd', (p / l).astype(v.dtype), vv)
    o = o.reshape(B, sp, H, Dh)[:, :S]
    lse = (m + jnp.log(l))[..., 0]
    lse = lse.transpose(0, 1, 4, 2, 3).reshape(B, sp, H)[:, :S]
    return o, lse

def hybrid_mixer(u, positions, w_in, conv_w, w_conv_out, w_attn_out, gate_bias, w_out):
    B, S, _ = u.shape
    sizes = [D_CONV, D_CONV, D_CONV, D_ATTN, D_ATTN, D_ATTN, D_MODEL, D_MODEL]
    split_points = [int(c) for c in np.cumsum(sizes)[:-1]]
    proj = u @ w_in
    b_gate, c_gate, xc, q, k, v, g_conv, g_attn = jnp.split(proj, split_points, axis=-1)

    z = c_gate * xc
    zp = jnp.pad(z, ((0, 0), (CONV_WIDTH - 1, 0), (0, 0)))
    conv = sum(conv_w[i] * zp[:, i:i + S] for i in range(CONV_WIDTH))
    y_conv = (b_gate * conv) @ w_conv_out

    q = partial_rotary(q.reshape(B, S, N_ATTN_HEADS, HEAD_DIM), positions)
    k = partial_rotary(k.reshape(B, S, N_ATTN_HEADS, HEAD_DIM), positions)
    v = v.reshape(B, S, N_ATTN_HEADS, HEAD_DIM)
    outs, lses = [], []
    for g, (window, dilation) in enumerate(DILATED_GROUPS):
        sl = slice(g * HEADS_PER_GROUP, (g + 1) * HEADS_PER_GROUP)
        o_g, lse_g = dilated_window_attention(q[:, :, sl], k[:, :, sl], v[:, :, sl], window, dilation)
        outs.append(o_g)
        lses.append(lse_g)
    wts = jax.nn.softmax(jnp.stack(lses, axis=0), axis=0)
    o = jnp.einsum('gbsh,gbshd->bshd', wts.astype(v.dtype), jnp.stack(outs, axis=0))
    y_attn = o.reshape(B, S, D_ATTN_OUT) @ w_attn_out

    merged = (jax.nn.sigmoid(g_conv + gate_bias[0]) * y_conv
              + jax.nn.sigmoid(g_attn + gate_bias[1]) * y_attn)
    return merged @ w_out

def peer_ffn(u, w_query, sub_keys, expert_down, expert_up):
    B, S, D = u.shape
    T = B * S
    xf = u.reshape(T, D)
    q = (xf @ w_query).reshape(T, PEER_HEADS, 2, PEER_D_HALF)
    s = jnp.einsum('thcd,hckd->thck', q, sub_keys, preferred_element_type=jnp.float32)
    top_s, top_i = lax.top_k(s, PEER_TOPK)
    cand_s = (top_s[:, :, 0, :, None] + top_s[:, :, 1, None, :]).reshape(T, PEER_HEADS, PEER_TOPK * PEER_TOPK)
    cand_i = (top_i[:, :, 0, :, None] * PEER_N_KEYS + top_i[:, :, 1, None, :]).reshape(T, PEER_HEADS, PEER_TOPK * PEER_TOPK)
    best_s, pos = lax.top_k(cand_s, PEER_TOPK)
    idx = jnp.take_along_axis(cand_i, pos, axis=-1)
    gates = jax.nn.softmax(best_s, axis=-1).astype(u.dtype)
    hk = PEER_HEADS * PEER_TOPK
    xr = xf.reshape(-1, PEER_CHUNK, D)
    ir = idx.reshape(-1, PEER_CHUNK, hk)
    gr = gates.reshape(-1, PEER_CHUNK, hk)

    def chunk(args):
        xc, ic, gc = args
        a = jax.nn.gelu(jnp.einsum('cd,ced->ce', xc, expert_down[ic]), approximate=False)
        return jnp.einsum('ce,ced->cd', gc * a, expert_up[ic])

    return lax.map(chunk, (xr, ir, gr)).reshape(B, S, D)

def first_inputs(seed: int = 0) -> dict:
    key = jax.random.key(seed)
    ks = jax.random.split(key, 16)
    f32 = jnp.float32
    d_in = 3 * D_CONV + 3 * D_ATTN + 2 * D_MODEL
    x = jax.random.normal(ks[0], (BATCH, SEQ, D_MODEL), f32)
    offset = jax.random.randint(ks[1], (BATCH, 1), 0, 1024, dtype=jnp.int32)
    positions = (offset + jnp.arange(SEQ, dtype=jnp.int32)[None, :]).astype(jnp.int32)
    norm_mix = 1.0 + 0.01 * jax.random.normal(ks[2], (DEPTH, D_MODEL), f32)
    w_in = jax.random.normal(ks[3], (DEPTH, D_MODEL, d_in), f32) * D_MODEL ** -0.5
    conv_w = jax.random.normal(ks[4], (DEPTH, CONV_WIDTH, D_CONV), f32) * CONV_WIDTH ** -0.5
    w_conv_out = jax.random.normal(ks[5], (DEPTH, D_CONV, D_MODEL), f32) * D_CONV ** -0.5
    w_attn_out = jax.random.normal(ks[6], (DEPTH, D_ATTN_OUT, D_MODEL), f32) * D_ATTN_OUT ** -0.5
    gate_bias = 0.01 * jax.random.normal(ks[7], (DEPTH, 2, D_MODEL), f32)
    w_out = jax.random.normal(ks[8], (DEPTH, D_MODEL, D_MODEL), f32) * D_MODEL ** -0.5
    norm_ffn = 1.0 + 0.01 * jax.random.normal(ks[9], (DEPTH, D_MODEL), f32)
    peer_w_query = jax.random.normal(ks[10], (DEPTH, D_MODEL, PEER_HEADS * PEER_D_QUERY), f32) * D_MODEL ** -0.5
    peer_sub_keys = jax.random.normal(ks[11], (DEPTH, PEER_HEADS, 2, PEER_N_KEYS, PEER_D_HALF), f32) * PEER_D_HALF ** -0.5
    peer_down = jax.random.normal(ks[12], (DEPTH, PEER_N_EXPERTS, D_MODEL), f32) * D_MODEL ** -0.5
    peer_up = jax.random.normal(ks[13], (DEPTH, PEER_N_EXPERTS, D_MODEL), f32) * PEER_HEADS ** -0.5
    final_norm = 1.0 + 0.01 * jax.random.normal(ks[14], (D_MODEL,), f32)
    return {"x": x, "positions": positions, "norm_mix": norm_mix, "w_in": w_in,
            "conv_w": conv_w, "w_conv_out": w_conv_out, "w_attn_out": w_attn_out,
            "gate_bias": gate_bias, "w_out": w_out, "norm_ffn": norm_ffn,
            "peer_w_query": peer_w_query, "peer_sub_keys": peer_sub_keys,
            "peer_down": peer_down, "peer_up": peer_up, "final_norm": final_norm}

def first_block(x, positions, norm_mix, w_in, conv_w, w_conv_out, w_attn_out, gate_bias, w_out,
              norm_ffn, peer_w_query, peer_sub_keys, peer_down, peer_up, final_norm):
    h = x
    for layer in range(DEPTH):
        h = h + hybrid_mixer(rms_norm(h, norm_mix[layer]), positions, w_in[layer], conv_w[layer],
                             w_conv_out[layer], w_attn_out[layer], gate_bias[layer], w_out[layer])
        h = h + peer_ffn(rms_norm(h, norm_ffn[layer]), peer_w_query[layer], peer_sub_keys[layer],
                         peer_down[layer], peer_up[layer])
    return rms_norm(h, final_norm)


DEPTH_2 = 2

N_A = DEPTH_2 // 2
N_B = DEPTH_2 - N_A
CONV_WIDTH_2 = 31
N_HEADS = 8
V_DIM = 2 * HEAD_DIM
QK_WIDTH = 2 * N_HEADS * HEAD_DIM
V_WIDTH = N_HEADS * V_DIM
N_BUCKETS = 32
MAX_DISTANCE = 128
Q_BLOCK = 128
N_EXPERTS = 16
N_GROUPS = 4
EXPERTS_PER_GROUP = N_EXPERTS // N_GROUPS
TOP_K = 2
D_EXPERT = 512
ALPHA = (2.0 * DEPTH_2) ** 0.25
BETA = (8.0 * DEPTH_2) ** -0.25
LN_EPS = 1e-5


def layer_norm(x, g, b):
    xf = x.astype(jnp.float32)
    mu = jnp.mean(xf, -1, keepdims=True)
    var = jnp.mean(jnp.square(xf - mu), -1, keepdims=True)
    return ((xf - mu) * lax.rsqrt(var + LN_EPS) * g.astype(jnp.float32) + b.astype(jnp.float32)).astype(x.dtype)

def conformer_conv(x, w_pw1, b_pw1, w_dw, b_dw, g, b, w_pw2, b_pw2):
    h = x @ w_pw1 + b_pw1
    a, gate = jnp.split(h, 2, axis=-1)
    h = a * jax.nn.sigmoid(gate)
    h = lax.conv_general_dilated(
        h, w_dw[:, None, :].astype(h.dtype), window_strides=(1,),
        padding=[(CONV_WIDTH_2 - 1, 0)],
        dimension_numbers=("NWC", "WIO", "NWC"),
        feature_group_count=D_MODEL) + b_dw
    h = jax.nn.silu(layer_norm(h, g, b))
    return h @ w_pw2 + b_pw2

def t5_bucket(n):
    n = jnp.maximum(n, 0)
    max_exact = N_BUCKETS // 2
    nf = jnp.maximum(n, 1).astype(jnp.float32)
    large = max_exact + (jnp.log(nf / max_exact) / math.log(MAX_DISTANCE / max_exact)
                         * (N_BUCKETS - max_exact)).astype(jnp.int32)
    large = jnp.minimum(large, N_BUCKETS - 1)
    return jnp.where(n < max_exact, n, large)

def diff_attention(x, k1, k2, v, w_q, lam_params, subln_g, w_o, rel_bias, layer_idx):
    bsz, seq, _ = x.shape
    n_blk = seq // Q_BLOCK
    lambda_init = 0.8 - 0.6 * math.exp(-0.3 * layer_idx)
    lp = lam_params.astype(jnp.float32)
    lam = jnp.exp(jnp.sum(lp[0] * lp[1])) - jnp.exp(jnp.sum(lp[2] * lp[3])) + lambda_init
    q = (x @ w_q).reshape(bsz, n_blk, Q_BLOCK, 2, N_HEADS, HEAD_DIM)
    q = jnp.transpose(q, (3, 1, 0, 4, 2, 5))
    scale = HEAD_DIM ** -0.5
    k_pos = jnp.arange(seq)

    def block(args):
        qb1, qb2, i = args
        q_pos = i * Q_BLOCK + jnp.arange(Q_BLOCK)
        rel = q_pos[:, None] - k_pos[None, :]
        bias = jnp.transpose(jnp.take(rel_bias, t5_bucket(rel), axis=0), (2, 0, 1)).astype(jnp.float32)
        causal = rel >= 0

        def probs(qb, k):
            s = jnp.einsum("bhqd,bhkd->bhqk", qb, k).astype(jnp.float32) * scale + bias
            return jax.nn.softmax(jnp.where(causal, s, -jnp.inf), axis=-1)

        a = probs(qb1, k1) - lam * probs(qb2, k2)
        return jnp.einsum("bhqk,bhkv->bhqv", a.astype(v.dtype), v)

    out = lax.map(block, (q[0], q[1], jnp.arange(n_blk)))
    out = jnp.transpose(out, (1, 0, 3, 2, 4)).reshape(bsz, seq, N_HEADS, V_DIM)
    of = out.astype(jnp.float32)
    of = of * lax.rsqrt(jnp.mean(jnp.square(of), -1, keepdims=True) + LN_EPS) * subln_g.astype(jnp.float32)
    of = of * (1.0 - lambda_init)
    return of.astype(x.dtype).reshape(bsz, seq, V_WIDTH) @ w_o

def grouped_moe(x, router_w, router_bias, w_gate, w_up, w_down):
    bsz, seq, d = x.shape
    x2 = x.reshape(-1, d)
    aff = jax.nn.sigmoid((x2 @ router_w).astype(jnp.float32))
    sel = (aff + router_bias.astype(jnp.float32)).reshape(-1, N_GROUPS, EXPERTS_PER_GROUP)
    grp_score = jnp.sum(lax.top_k(sel, 2)[0], -1)
    g_idx = jnp.argmax(grp_score, -1)
    in_grp = jnp.take_along_axis(sel, g_idx[:, None, None], axis=1)[:, 0]
    _, local = lax.top_k(in_grp, TOP_K)
    e_idx = g_idx[:, None] * EXPERTS_PER_GROUP + local
    w = jnp.take_along_axis(aff, e_idx, -1)
    w = w / jnp.sum(w, -1, keepdims=True)
    gates = jnp.sum(jax.nn.one_hot(e_idx, N_EXPERTS, dtype=jnp.float32) * w[..., None], axis=1)

    def step(acc, ew):
        g_e, wg_e, wu_e, wd_e = ew
        h = jax.nn.silu(x2 @ wg_e) * (x2 @ wu_e)
        return acc + (h @ wd_e) * g_e[:, None].astype(x2.dtype), None

    out, _ = lax.scan(step, jnp.zeros_like(x2), (gates.T, w_gate, w_up, w_down))
    return out.reshape(bsz, seq, d)

def second_inputs(seed: int = 0) -> dict:
    key = jax.random.key(seed)
    ks = jax.random.split(key, 32)
    nrm = jax.random.normal
    D, f32 = D_MODEL, jnp.float32
    w_kv_k = nrm(ks[9], (D, QK_WIDTH), f32) * D ** -0.5
    w_kv_v = nrm(ks[10], (D, V_WIDTH), f32) * D ** -0.5 * BETA
    return {
        "x": nrm(ks[0], (BATCH, SEQ, D), f32),
        "a_w_pw1": nrm(ks[1], (N_A, D, 2 * D), f32) * D ** -0.5,
        "a_b_pw1": 0.02 * nrm(ks[2], (N_A, 2 * D), f32),
        "a_w_dw": nrm(ks[3], (N_A, CONV_WIDTH_2, D), f32) * CONV_WIDTH_2 ** -0.5,
        "a_b_dw": 0.02 * nrm(ks[4], (N_A, D), f32),
        "a_ln_g": 1.0 + 0.02 * nrm(ks[5], (N_A, D), f32),
        "a_ln_b": 0.02 * nrm(ks[6], (N_A, D), f32),
        "a_w_pw2": nrm(ks[7], (N_A, D, D), f32) * D ** -0.5 * BETA,
        "a_b_pw2": 0.02 * nrm(ks[8], (N_A, D), f32),
        "w_kv": jnp.concatenate([w_kv_k, w_kv_v], axis=1),
        "b_w_q": nrm(ks[11], (N_B, D, QK_WIDTH), f32) * D ** -0.5,
        "b_lambda": 0.1 * nrm(ks[12], (N_B, 4, HEAD_DIM), f32),
        "b_subln_g": 1.0 + 0.02 * nrm(ks[13], (N_B, V_DIM), f32),
        "b_w_o": nrm(ks[14], (N_B, V_WIDTH, D), f32) * V_WIDTH ** -0.5 * BETA,
        "rel_bias": 0.5 * nrm(ks[15], (N_BUCKETS, N_HEADS), f32),
        "ln_mix_g": 1.0 + 0.02 * nrm(ks[16], (DEPTH_2, D), f32),
        "ln_mix_b": 0.02 * nrm(ks[17], (DEPTH_2, D), f32),
        "ln_ffn_g": 1.0 + 0.02 * nrm(ks[18], (DEPTH_2, D), f32),
        "ln_ffn_b": 0.02 * nrm(ks[19], (DEPTH_2, D), f32),
        "router_w": nrm(ks[20], (D, N_EXPERTS), f32) * D ** -0.5,
        "router_bias": 0.01 * nrm(ks[21], (N_EXPERTS,), f32),
        "moe_w_gate": nrm(ks[22], (DEPTH_2, N_EXPERTS, D, D_EXPERT), f32) * D ** -0.5,
        "moe_w_up": nrm(ks[23], (DEPTH_2, N_EXPERTS, D, D_EXPERT), f32) * D ** -0.5,
        "moe_w_down": nrm(ks[24], (DEPTH_2, N_EXPERTS, D_EXPERT, D), f32) * D_EXPERT ** -0.5 * BETA,
    }

def second_block(x, a_w_pw1, a_b_pw1, a_w_dw, a_b_dw, a_ln_g, a_ln_b, a_w_pw2, a_b_pw2,
              w_kv, b_w_q, b_lambda, b_subln_g, b_w_o, rel_bias,
              ln_mix_g, ln_mix_b, ln_ffn_g, ln_ffn_b,
              router_w, router_bias, moe_w_gate, moe_w_up, moe_w_down):
    bsz, seq, _ = x.shape
    k1 = k2 = v = None
    for l in range(DEPTH_2):
        if l < N_A:
            mix = conformer_conv(x, a_w_pw1[l], a_b_pw1[l], a_w_dw[l], a_b_dw[l],
                                 a_ln_g[l], a_ln_b[l], a_w_pw2[l], a_b_pw2[l])
        else:
            if l == N_A:
                kv = x @ w_kv
                k = kv[..., :QK_WIDTH].reshape(bsz, seq, 2, N_HEADS, HEAD_DIM)
                k = jnp.transpose(k, (2, 0, 3, 1, 4))
                k1, k2 = k[0], k[1]
                v = jnp.transpose(kv[..., QK_WIDTH:].reshape(bsz, seq, N_HEADS, V_DIM), (0, 2, 1, 3))
            j = l - N_A
            mix = diff_attention(x, k1, k2, v, b_w_q[j], b_lambda[j], b_subln_g[j], b_w_o[j], rel_bias, l)
        x = layer_norm(ALPHA * x + mix, ln_mix_g[l], ln_mix_b[l])
        ffn = grouped_moe(x, router_w, router_bias, moe_w_gate[l], moe_w_up[l], moe_w_down[l])
        x = layer_norm(ALPHA * x + ffn, ln_ffn_g[l], ln_ffn_b[l])
    return x


def setup_inputs(seed=0):
    out = dict(first_inputs(seed))
    for name, value in second_inputs(seed + 1).items():
        if name != "x":
            out[name + "_2"] = value
    return out


def reference(
    x, positions, norm_mix, w_in, conv_w, w_conv_out, w_attn_out, gate_bias, w_out, norm_ffn,
    peer_w_query, peer_sub_keys, peer_down, peer_up, final_norm, a_w_pw1_2, a_b_pw1_2, a_w_dw_2,
    a_b_dw_2, a_ln_g_2, a_ln_b_2, a_w_pw2_2, a_b_pw2_2, w_kv_2, b_w_q_2, b_lambda_2,
    b_subln_g_2, b_w_o_2, rel_bias_2, ln_mix_g_2, ln_mix_b_2, ln_ffn_g_2, ln_ffn_b_2,
    router_w_2, router_bias_2, moe_w_gate_2, moe_w_up_2, moe_w_down_2,
):
    x = first_block(
        x, positions, norm_mix, w_in, conv_w, w_conv_out, w_attn_out, gate_bias, w_out,
        norm_ffn, peer_w_query, peer_sub_keys, peer_down, peer_up, final_norm,
    )
    return second_block(
        x, a_w_pw1_2, a_b_pw1_2, a_w_dw_2, a_b_dw_2, a_ln_g_2, a_ln_b_2, a_w_pw2_2, a_b_pw2_2,
        w_kv_2, b_w_q_2, b_lambda_2, b_subln_g_2, b_w_o_2, rel_bias_2, ln_mix_g_2, ln_mix_b_2,
        ln_ffn_g_2, ln_ffn_b_2, router_w_2, router_bias_2, moe_w_gate_2, moe_w_up_2,
        moe_w_down_2,
    )


_drawn_inputs = setup_inputs


def setup_inputs(seed=0):
    import zlib

    import numpy as np

    out = dict(_drawn_inputs(seed))
    spreads = {}
    factors = {'gate_bias': 3.278, 'a_b_pw1_2': 2.821, 'b_subln_g_2': 5.091}
    for name, (base, spread) in spreads.items():
        noise = np.random.default_rng([zlib.crc32(name.encode()), seed]).standard_normal(out[name].shape)
        drawn = base * np.exp(spread * noise) if base else spread * noise
        out[name] = __import__('jax').numpy.asarray(drawn.astype(out[name].dtype))
    for name, factor in factors.items():
        out[name] = (out[name] * factor).astype(out[name].dtype)
    return out
```

```python
import math
from contextlib import ExitStack

import concourse.bass as bass
import numpy as np
from concourse import mybir
from concourse.alu_op_type import AluOpType as ALU

F32 = mybir.dt.float32
BF16 = mybir.dt.bfloat16
I32 = mybir.dt.int32
U32 = mybir.dt.uint32
ACT = mybir.ActivationFunctionType
AX = mybir.AxisListType

P = 128
T = 256
D = 1024
DT = D // P
TT = T // P
HALF = 2 * T

HEADS = 8
GROUPS = 3
DILATIONS = (1, 4, 16)
STEPS = 128
HD = 64
ROT = HD // 4
ROPE_THETA = 500000.0
PH = 8
NK = 128
TOPK = 16
SLOTS_T = PH * TOPK
RMS_EPS = 1e-6
TAPS = 31
BUCKETS = 32
MAX_DISTANCE = 128
NE = 16
NG = 4
EPG = NE // NG
FE = 512
LN_EPS = 1e-5
ALPHA = 4.0 ** 0.25
LAMBDA_INIT = 0.8 - 0.6 * math.exp(-0.3)
NEG = -1e30

CW = 2048
RING = 6
_counts = [("c", 4), ("xc", 4), ("b", 4), ("q", 6), ("k", 6), ("v", 6), ("gc", 4), ("ga", 4),
           ("conv_out", 4), ("attn_out", 4), ("w_out", 4), ("wq", 8), ("down", 64), ("up", 64),
           ("pw1", 8), ("pw2", 4), ("moe0", 6 * NE), ("k2", 4), ("v2", 4), ("q2", 4),
           ("w_o", 4), ("moe1", 6 * NE)]
C0, _n = {}, 0
for _name, _k in _counts:
    C0[_name] = _n
    _n += _k
CHUNKS = _n

UNIT_BANKS = 3
_unit_counts = [(n, k) for n, k in _counts if n not in ("up", "moe0", "moe1")]
_unit_counts.insert([n for n, _ in _unit_counts].index("down"), ("keyscore", 8))
U0, _n = {}, 0
for _name, _k in _unit_counts:
    U0[_name] = _n
    _n += _k

_vecs = [("norm_mix", 8), ("conv_w", 24), ("gate_bias", 16), ("norm_ffn", 8), ("final_norm", 8),
         ("b_pw1", 16), ("w_dw", TAPS * 8), ("b_dw", 8), ("ln_g", 8), ("ln_b", 8), ("b_pw2", 8),
         ("ln_mix_g", 16), ("ln_mix_b", 16), ("ln_ffn_g", 16), ("ln_ffn_b", 16), ("subln_g", 1)]
V0, _n = {}, 0
for _name, _k in _vecs:
    V0[_name] = _n
    _n += _k
VECS = _n

_consts = [("ident", P), ("rot", P), ("iota", P), ("freq", 1), ("lower", EPG * EPG)]
K0, _n = {}, 0
for _name, _k in _consts:
    K0[_name] = _n
    _n += _k
CONSTS = _n
RELS = 384


def constants():
    pack = np.zeros((P, CONSTS), np.float32)
    pack[:, K0["ident"]:K0["ident"] + P] = np.eye(P)
    rot = np.zeros((P, P), np.float32)
    freq = np.zeros((P,), np.float32)
    half = ROT // 2
    inv = (ROPE_THETA ** (-np.arange(half) * (2.0 / ROT))).astype(np.float32)
    for m in range(P):
        d = m % HD
        if d < half:
            rot[m + half, m] = -1.0
        elif d < ROT:
            rot[m - half, m] = 1.0
        if d < ROT:
            freq[m] = inv[d % half]
    pack[:, K0["rot"]:K0["rot"] + P] = rot
    pack[:, K0["iota"]:K0["iota"] + P] = np.arange(P)[None]
    pack[:, K0["freq"]] = freq
    lower = np.tril(np.ones((EPG, EPG), np.float32), -1)
    pack[:, K0["lower"]:K0["lower"] + EPG * EPG] = lower.reshape(-1)[None]
    rel = P + np.arange(P)[:, None] - np.arange(T)[None]
    mask = np.stack([np.where((rel >= 0) & (rel % r == 0) & (rel <= STEPS * r), 0.0, NEG)
                     for r in DILATIONS], 1)
    rels = (T - 1) - np.arange(RELS)
    exact = BUCKETS // 2
    nf = np.maximum(rels, 1).astype(np.float32)
    large = exact + (np.log(nf / exact) / math.log(MAX_DISTANCE / exact)
                     * (BUCKETS - exact)).astype(np.int32)
    bucket = np.where(rels < exact, np.maximum(rels, 0), np.minimum(large, BUCKETS - 1))
    onehot = np.zeros((BUCKETS + 1, RELS), np.float32)
    onehot[bucket, np.arange(RELS)] = 1.0
    onehot[BUCKETS] = np.where(rels >= 0, 0.0, NEG)
    pick = np.zeros((NE, NE, P), np.float32)
    for e in range(NE):
        pick[e, e] = 1.0
    return {"consts": pack, "mask": mask.astype(np.float32).reshape(P, -1), "onehot": onehot,
            "pick": pick.reshape(NE, NE * P)}


def build(nc, t_x, t_w, t_vec, t_const, t_mask, t_onehot, t_pick, t_pos, t_keys, t_router,
          t_rbias, t_lam, t_rel, t_rows, t_out, dbg=None):
    ctx = ExitStack()
    with ctx:
        def sb(name, shape, dt=F32):
            return ctx.enter_context(nc.sbuf_tensor(name, shape, dt))

        def sem(name):
            return ctx.enter_context(nc.semaphore(name))

        ring = sb("ring", [P, RING, CW])
        big = sb("big", [P, NK * T])
        h = sb("h", [P, DT, T])
        u = sb("u", [P, DT, T])
        const = sb("const", [P, CONSTS])
        vec = sb("vec", [P, VECS])
        ones_d = sb("ones_d", [P, P])
        zeros = sb("zeros", [P, HALF], BF16)
        root = sb("root", [P, T])
        slot_t = sb("slot_t", [P, 3, T])
        router = sb("router", [P, DT, NE])
        rbias = sb("rbias", [P, NE])
        small = sb("small", [P, 384])
        eps = sb("eps", [P, 2])
        bank = [ctx.enter_context(nc.psum_tensor(f"bank{i}", [P, HALF], F32)) for i in range(8)]

        def C(name):
            return const[:, K0[name]:K0[name] + dict(_consts)[name]]

        def V(name, k):
            return vec[:, V0[name] + k:V0[name] + k + 1]

        ident = C("ident")

        class Region:

            def __init__(self, at, end=NK * T):
                self.at, self.end = at, end

            def take(self, *shape):
                n = math.prod(shape)
                assert self.at + n <= self.end, (self.at, n, self.end)
                v = big[:, self.at:self.at + n]
                self.at += n
                names = "abcd"[:len(shape)]
                if len(shape) == 1:
                    return v
                return v.rearrange(f"p ({' '.join(names)}) -> p {' '.join(names)}",
                                   **{c: s for c, s in zip(names[1:], shape[1:])})

        r1 = Region(0)
        cgate = r1.take(DT, T)
        z = r1.take(DT, T + 2)
        conv = r1.take(DT, T)
        qk = r1.take(2 * GROUPS * 4, T)
        v1 = r1.take(TT, GROUPS * HEADS * HD)
        sig_c = r1.take(DT, T)
        sig_a = r1.take(DT, T)
        merged = r1.take(DT, T)
        o_t = r1.take(4, T)
        cos_t = r1.take(T)
        sin_t = r1.take(T)
        ang = r1.take(T)
        turn = r1.take(T)
        rot_tmp = r1.take(2, T)
        mask = r1.take(GROUPS, T)
        sc1 = r1.take(2, GROUPS, T)
        pr1 = r1.take(2, GROUPS, T)
        pt1 = r1.take(2, GROUPS * T)
        sq1 = cgate
        rows = qk.rearrange("p a b -> p (a b)")[:, 0:8 * RELS].rearrange("p (h r) -> p h r", h=8)
        act = big[:, :].rearrange("p (i t) -> p i t", t=T)
        rp = Region(0)
        pq = rp.take(PH * 2, T)
        keys = rp.take(PH * 2, P)
        TILES_BEFORE = 72
        rk = Region(TILES_BEFORE * T)
        score = rk.take(TT, PH * 2, NK)
        cand = rk.take(PH, TOPK * TOPK)
        match = rk.take(PH, TOPK, TOPK)
        top_v = rk.take(TT, PH * 2, TOPK)
        top_i = rk.take(TT, PH * 2, TOPK)
        top_f = rk.take(TT, PH * 2, TOPK)
        best = rk.take(TT, PH, TOPK)
        best_i = rk.take(TT, PH, TOPK)
        pos_a = rk.take(TT, SLOTS_T)
        pos_b = rk.take(TT, SLOTS_T)
        pos_f = rk.take(2, TT, SLOTS_T)
        slot = rk.take(3, TT, SLOTS_T)
        r2 = Region(0)
        pre = r2.take(DT, T)
        cen = r2.take(DT, T)
        nrm = r2.take(DT, T)
        sq2 = r2.take(DT, T)
        glu = r2.take(DT, T + TAPS - 1)
        sg2 = r2.take(2, T)
        gate_b = r2.take(NE, T)
        silu = r2.take(2, HALF)
        hid = r2.take(4, T)
        prod = r2.take(2, T)
        k2 = r2.take(DT, T)
        v2 = r2.take(TT, D)
        q2 = r2.take(DT, T)
        relb = r2.take(HEADS, T)
        sc2 = r2.take(2, 2, T)
        pr2 = r2.take(2, 2, T)
        pt2 = r2.take(2, T)
        o_tok = glu[:, 0:DT, 0:T]
        at_out = k2
        pick = u[:, :, :].rearrange("p a b -> p (a b)")
        neg_max = small[:, 0:4]
        denom = small[:, 4:8]
        rden = small[:, 8:12]
        lam = small[:, 12:16]
        sumsq = small[:, 16:32]
        sub_g = small[:, 32:33]
        mx8 = small[:, 33:34]
        aff = small[:, 64:96].rearrange("p (a b) -> p a b", a=TT)
        sel = small[:, 96:128].rearrange("p (a b) -> p a b", a=TT)
        top2 = small[:, 128:160].rearrange("p (a b) -> p a b", a=TT)
        rank = small[:, 160:192]
        gscore = small[:, 192:200]
        grank = small[:, 200:208]
        gates = small[:, 208:240].rearrange("p (a b) -> p a b", a=TT)
        wsum = small[:, 240:242]
        gsum = small[:, 256:272].rearrange("p (a b) -> p a b", a=TT)
        gsel = small[:, 272:304].rearrange("p (a b) -> p a b", a=TT)
        lamp = cen
        gate_t = sb("gate_t", [NE, T])

        w_ready = [sem(f"w_ready{i}") for i in range(RING)]
        chunk_done = sem("chunk_done")
        unit_free = [sem(f"unit_free{i}") for i in range(UNIT_BANKS)]
        loaded = sem("loaded")
        x_loaded = sem("x_loaded")
        keys_loaded = sem("keys_loaded")
        two_loaded = sem("two_loaded")
        set_up = sem("set_up")
        rows_ready = sem("rows_ready")
        rows_copied = sem("rows_copied")
        rows_stored = sem("rows_stored")
        stat_in = sem("stat_in")
        stat_out = sem("stat_out")
        centred = sem("centred")
        root_ready = sem("root_ready")
        scaled = sem("scaled")
        norm_done = sem("norm_done")
        angles_ready = sem("angles_ready")
        rope_ready = sem("rope_ready")
        rot_ready = sem("rot_ready")
        rot_done = sem("rot_done")
        s_ready = sem("s_ready")
        s_read = sem("s_read")
        max_ready = sem("max_ready")
        exp_done = sem("exp_done")
        p_ready = sem("p_ready")
        t_ready = sem("t_ready")
        pt_ready = sem("pt_ready")
        pv_done = sem("pv_done")
        o_done = sem("o_done")
        key_s = sem("key_s")
        best_ready = sem("best_ready")
        best_exp = sem("best_exp")
        slots_ready = sem("slots_ready")
        slots_t = sem("slots_t")
        slots_copied = sem("slots_copied")
        onehot_ready = [sem(f"onehot_ready{i}") for i in range(2)]
        scattered = [sem(f"scattered{i}") for i in range(2)]
        gated = [sem(f"gated{i}") for i in range(2)]
        acc_zero = sem("acc_zero")
        act_read = sem("act_read")
        res_done = sem("res_done")
        glu_sig = sem("glu_sig")
        mix_b = sem("mix_b")
        logits = sem("logits")
        affin = sem("affin")
        gates_ready = sem("gates_ready")
        gates_t = sem("gates_t")
        gates_copied = sem("gates_copied")
        gb_ready = sem("gb_ready")
        gb_done = sem("gb_done")
        silu_done = sem("silu_done")
        hid_done = sem("hid_done")
        lam_exp = sem("lam_exp")
        lam_sum = sem("lam_sum")
        sub_sum = sem("sub_sum")
        sub_root = sem("sub_root")
        sub_scaled = sem("sub_scaled")
        sub_t = sem("sub_t")
        sub_out = sem("sub_out")
        out_stored = sem("out_stored")
        dve_step = sem("dve_step")
        act_step = sem("act_step")

        NORMS = {n: i + 1 for i, n in enumerate(
            ["mix", "ffn", "final", "conv", "mix0", "ffn0", "mix1", "ffn1"])}
        STATS = {"mix": 1, "ffn": 2, "final": 3, "conv": 4, "mix0": 6, "ffn0": 8, "mix1": 10, "ffn1": 12}
        ROOTS = NORMS
        LNS = {"conv": 1, "mix0": 2, "ffn0": 3, "mix1": 4, "ffn1": 5}
        RES = {"mixer": 1, "experts": 2, "pw2": 3, "moe0": 4, "w_o": 5, "moe1": 6}

        def unit_bank(unit):
            return bank[unit % UNIT_BANKS]

        def evacuated(eng, unit):
            eng.wait_ge(unit_free[unit % UNIT_BANKS], unit // UNIT_BANKS + 1)

        def computed(eng, name, j):
            eng.wait_ge(chunk_done, C0[name] + j + 1)

        def o_rows(qt):
            return (cen if qt == 0 else nrm).rearrange("p a b -> p (a b)")[:, 0:D]

        block = ctx.enter_context(nc.Block())

        @block.sync
        def _(sp):
            def load(chunk, slot):
                sp.dma_start(ring[:, slot, :].unsqueeze(1),
                             t_w[bass.ds(chunk, 1)].rearrange("c p n -> p c n"))\
                    .then_inc(w_ready[slot], 16)

            for slot in range(RING):
                load(slot, slot)
            with sp.Fori(1, CHUNKS // RING) as turn_:
                for slot in range(RING):
                    sp.wait_ge(chunk_done, (turn_ - 1) * RING + slot + 1)
                    load(turn_ * RING + slot, slot)
            for slot in range(CHUNKS % RING):
                last = CHUNKS // RING * RING
                sp.wait_ge(chunk_done, last - RING + slot + 1)
                load(last + slot, slot)
            sp.wait_ge(norm_done, NORMS["ffn1"])
            sp.dma_start(t_out, h[:, :, :]).then_inc(out_stored, 16)
            sp.wait_ge(out_stored, 16)

        @block.gpsimd
        def _(pool):
            pool.dma_start(h[:, :, :], t_x).then_inc(x_loaded, 16)
            pool.dma_start(const[:, :], t_const).then_inc(loaded, 16)
            pool.dma_start(vec[:, :], t_vec).then_inc(loaded, 16)
            pool.dma_start(ang.bitcast(I32), t_pos.partition_broadcast(P)).then_inc(loaded, 16)
            pool.dma_start(mask, t_mask.rearrange("p (g k) -> p g k", g=GROUPS)).then_inc(loaded, 16)
            pool.dma_start(u[0:BUCKETS + 1, 0, :], t_onehot[:, 0:T]).then_inc(loaded, 16)
            pool.dma_start(u[0:BUCKETS + 1, 1, 0:RELS - T], t_onehot[:, T:RELS]).then_inc(loaded, 16)
            nc.gpsimd.memset(u[0:BUCKETS + 1, 2, 0:HEADS], 1.0).then_inc(set_up, 1)
            pool.wait_ge(set_up, 1)
            pool.dma_start(u[0:BUCKETS, 2, 0:HEADS], t_rel).then_inc(loaded, 16)
            pool.dma_start(router[:, :, :], t_router).then_inc(loaded, 16)
            pool.dma_start(rbias[:, :], t_rbias.partition_broadcast(P)).then_inc(loaded, 16)
            nc.gpsimd.memset(ones_d[:, :], 1.0 / D).then_inc(set_up, 1)
            nc.gpsimd.memset(zeros[:, :], 0.0).then_inc(set_up, 1)
            nc.gpsimd.memset(eps[:, 0:1], RMS_EPS).then_inc(set_up, 1)
            nc.gpsimd.memset(eps[:, 1:2], LN_EPS).then_inc(set_up, 1)
            nc.gpsimd.memset(z[:, :, 0:2], 0.0).then_inc(set_up, 1)
            pool.wait_ge(rows_copied, HEADS)
            pool.dma_start(t_rows.rearrange("h p r -> p h r"), rows).then_inc(rows_stored, 16)
            pool.wait_ge(norm_done, NORMS["ffn"])
            pool.dma_start(keys, t_keys).then_inc(keys_loaded, 16)
            pool.wait_ge(norm_done, NORMS["final"])
            pool.wait_ge(rows_stored, 16)
            for hd in range(HEADS):
                row = t_rows[hd].rearrange("p r -> (p r)")
                skew = row[P - 1:P - 1 + P * (RELS - 1)].rearrange("(p r) -> p r", r=RELS - 1)
                pool.dma_start(relb[:, hd, :], skew[:, 0:T]).then_inc(two_loaded, 16)
            pool.dma_start(lamp[:, 0, :], t_lam.partition_broadcast(P)).then_inc(two_loaded, 16)
            pool.dma_start(pick[0:NE, :], t_pick).then_inc(two_loaded, 16)

        @block.tensor
        def _(pe):
            def free_unit(unit, turns=0):
                if unit >= UNIT_BANKS:
                    pe.wait_ge(unit_free[unit % UNIT_BANKS], turns + unit // UNIT_BANKS)

            def arrived(chunk, turns=0):
                pe.wait_ge(w_ready[chunk % RING], (turns + chunk // RING + 1) * 16)

            def project(name, j, src, kt=DT, turns=0, unit_turns=0):
                chunk, unit = C0[name] + j, U0[name] + j
                w = ring[:, chunk % RING, 0:kt * 256].rearrange("p (k n) -> p k n", k=kt)
                free_unit(unit, unit_turns)
                arrived(chunk, turns)
                for n in range(2):
                    for k in range(kt):
                        last = nc.tensor.matmul(unit_bank(unit)[:, n * T:(n + 1) * T],
                                                w[:, k, n * P:(n + 1) * P], src[:, k, :],
                                                start=(k == 0), stop=(k == kt - 1))
                last.then_inc(chunk_done, 1)

            def project_rows(name, j, src):
                chunk, unit = C0[name] + j, U0[name] + j
                w = ring[:, chunk % RING, :].rearrange("p (k n) -> p k n", k=DT)
                free_unit(unit)
                arrived(chunk)
                for n in range(TT):
                    for k in range(DT):
                        last = nc.tensor.matmul(unit_bank(unit)[:, n * T:(n + 1) * T],
                                                src[:, k, n * P:(n + 1) * P], w[:, k, :],
                                                start=(k == 0), stop=(k == DT - 1))
                last.then_inc(chunk_done, 1)

            def mean(n, src):
                pe.wait_ge(stat_in, n)
                for k in range(DT):
                    last = nc.tensor.matmul(bank[3][:, 0:T], ones_d[:, :], src[:, k, :],
                                            start=(k == 0), stop=(k == DT - 1))
                last.then_inc(stat_out, 1)

            pe.wait_ge(loaded, 9 * 16)
            pe.wait_ge(set_up, 6)
            for hd in range(HEADS):
                lhs = u[0:BUCKETS + 1, 2, hd:hd + 1].broadcast_to([BUCKETS + 1, P])
                nc.tensor.matmul(bank[hd][:, 0:T], lhs, u[0:BUCKETS + 1, 0, :], start=True, stop=True)
                nc.tensor.matmul(bank[hd][:, T:RELS], lhs, u[0:BUCKETS + 1, 1, 0:RELS - T],
                                 start=True, stop=True).then_inc(rows_ready, 1)
            pe.wait_ge(rows_copied, HEADS)
            mean(STATS["mix"], sq1)
            pe.wait_ge(norm_done, NORMS["mix"])
            for name in ("c", "xc", "b"):
                for j in range(4):
                    project(name, j, u)

            def rotate(j):
                evacuated(pe, U0["q"] + j)
                if j >= 2:
                    pe.wait_ge(rot_done, j - 1)
                nc.tensor.matmul(bank[3 + j % 2][:, :], C("rot"), qk[:, 2 * j:2 * j + 2, :],
                                 start=True, stop=True).then_inc(rot_ready, 1)

            for j in range(12):
                project("q", j, u) if j < 6 else project("k", j - 6, u)
                if j >= 1:
                    rotate(j - 1)
            project_rows("v", 0, u)
            rotate(11)
            for j in range(1, 6):
                project_rows("v", j, u)
            for name in ("gc", "ga"):
                for j in range(4):
                    project(name, j, u)
            evacuated(pe, U0["b"] + 3)
            for j in range(4):
                project("conv_out", j, conv)

            pe.wait_ge(rot_done, 12)
            for b_ in range(6):
                evacuated(pe, U0["v"] + b_)
            tiles = [(hd, qt) for hd in range(HEADS) for qt in range(TT)]

            def scores(i):
                hd, qt = tiles[i]
                row, n = hd % 2 * HD, (qt + 1) * P
                if i >= 2:
                    pe.wait_ge(s_read, i - 1)
                for g in range(GROUPS):
                    ft = g * 4 + hd // 2
                    out = bank[3 + i % 2 * 2 + g // 2][:, g % 2 * T:g % 2 * T + n]
                    last = nc.tensor.matmul(out, qk[row:row + HD, ft, qt * P:(qt + 1) * P],
                                            qk[row:row + HD, 12 + ft, 0:n], start=True, stop=True)
                last.then_inc(s_ready, 1)

            tb = [(0, 1), (2, 7)]

            def blocks(i):
                return [(g, kt) for g in range(GROUPS) for kt in range(tiles[i][1] + 1)]

            def transposes(i):
                pe.wait_ge(p_ready, i + 1)
                if i >= 2:
                    pe.wait_ge(o_done, i - 1)
                for n, (g, kt) in enumerate(blocks(i)):
                    last = nc.tensor.transpose(bank[tb[i % 2][n // 4]][:, n % 4 * P:n % 4 * P + P],
                                               pr1[:, i % 2, g, kt * P:(kt + 1) * P], ident)
                last.then_inc(t_ready, 1)

            def values(i):
                hd, qt = tiles[i]
                pe.wait_ge(pt_ready, i + 1)
                bl = blocks(i)
                for n, (g, kt) in enumerate(bl):
                    at = (g * HEADS + hd // 2 * 2) * HD
                    last = nc.tensor.matmul(bank[tb[i % 2][1]][:, T:T + P], v1[:, kt, at:at + P],
                                            pt1[:, i % 2, n * P:(n + 1) * P],
                                            start=(n == 0), stop=(n == len(bl) - 1))
                last.then_inc(pv_done, 1)

            for unit in range(U0["attn_out"] - UNIT_BANKS, U0["attn_out"]):
                evacuated(pe, unit)
            scores(0)
            for i in range(len(tiles)):
                if i + 1 < len(tiles):
                    scores(i + 1)
                if i >= 1:
                    values(i - 1)
                transposes(i)
            values(len(tiles) - 1)

            pe.wait_ge(o_done, len(tiles))
            for j in range(4):
                project("attn_out", j, o_t, kt=4)
            evacuated(pe, U0["attn_out"] + 3)
            evacuated(pe, U0["attn_out"] + 2)
            for j in range(4):
                project("w_out", j, merged)
            mean(STATS["ffn"], sq1)
            pe.wait_ge(norm_done, NORMS["ffn"])
            for j in range(8):
                project("wq", j, u)
            pe.wait_ge(keys_loaded, 16)
            for b_ in range(3):
                evacuated(pe, U0["wq"] + 5 + b_)
            for j in range(8):
                tt, part = j // 4, j % 4
                free_unit(U0["keyscore"] + j)
                for c in range(4):
                    last = nc.tensor.matmul(unit_bank(U0["keyscore"] + j)[:, c * NK:(c + 1) * NK],
                                            pq[:, part * 4 + c, tt * P:(tt + 1) * P],
                                            keys[:, part * 4 + c, :], start=True, stop=True)
                last.then_inc(key_s, 1)
            with pe.Fori(0, 6) as it:
                for j in range(6):
                    project("down", j, u, turns=it, unit_turns=it * 2)
            pe.wait_ge(slots_ready, 1)
            for n in range(3):
                for tt in range(TT):
                    last = nc.tensor.transpose(bank[4 + n][:, tt * P:(tt + 1) * P],
                                               slot[:, n, tt, :], ident)
                last.then_inc([scattered[0], scattered[1], slots_t][n], 1)
            with pe.Fori(6, 10) as it:
                for j in range(6):
                    project("down", j, u, turns=it, unit_turns=it * 2)
            for j in range(60, 64):
                project("down", j, u)
            pe.wait_ge(slots_copied, 1)
            with pe.Fori(0, T // 8) as it:
                for half in range(2):
                    pe.wait_ge(onehot_ready[half], it + 1)
                    pe.wait_ge(gated[half], it + 1)
                    out = bank[4 + half][:, :].rearrange("p (i t) -> p t i", t=4)
                    for tk in range(4):
                        a = u[:, half * 4 + tk // 2, tk % 2 * P:tk % 2 * P + P]
                        b = u[:, half * 4 + 2 + tk // 2, tk % 2 * P:tk % 2 * P + P]
                        last = nc.tensor.matmul(out[:, tk, :], b, a, start=True, stop=True)
                    last.then_inc(scattered[half], 1)
            for half in range(2):
                pe.wait_ge(gated[half], T // 8 + 1)

            def zero_acc():
                for b_ in range(4, 8):
                    nc.tensor.matmul(bank[b_][:, :], zeros[:, 0:P], zeros[:, :],
                                     start=True, stop=False, skip_group_check=True)

            def accumulate(chunk, src, turns=0, final=False):
                w = ring[:, chunk % RING, :].rearrange("p (k n) -> p k n", k=2)
                arrived(chunk, turns)
                for k in range(2):
                    for n in range(DT):
                        last = nc.tensor.matmul(bank[4 + n // 2][:, n % 2 * T:n % 2 * T + T],
                                                w[:, k, n * P:(n + 1) * P], src[k],
                                                start=False, stop=(final and k == 1 and n % 2 == 1),
                                                skip_group_check=True)
                last.then_inc(chunk_done, 1)

            zero_acc()
            with pe.Fori(0, 10) as it:
                for j in range(6):
                    at = (it * 12 + 2 * j)
                    accumulate(C0["up"] + j, [act[:, bass.ds(at + k, 1), :].squeeze(1)
                                              for k in range(2)], turns=it)
            for j in range(60, 64):
                accumulate(C0["up"] + j, [act[:, 2 * j + k, :] for k in range(2)], final=(j == 63))
            mean(STATS["final"], sq2)

            pe.wait_ge(norm_done, NORMS["final"])
            for j in range(8):
                project("pw1", j, h)
            mean(STATS["conv"], pre)
            mean(STATS["conv"] + 1, sq2)
            pe.wait_ge(norm_done, NORMS["conv"])
            for j in range(4):
                project("pw2", j, cen)

            def layer_norm(name):
                mean(STATS[name], pre)
                mean(STATS[name] + 1, sq2)
                pe.wait_ge(norm_done, NORMS[name])

            def experts(layer):
                c0 = C0[f"moe{layer}"]
                halves = 2 * NE * layer

                def up_half(j, half, turns, done):
                    for n in range(2):
                        chunk = c0 + j + n
                        w = ring[:, chunk % RING, :].rearrange("p (k n) -> p k n", k=DT)
                        arrived(chunk, turns)
                        if n == 0 and done is not None:
                            pe.wait_ge(hid_done, done)
                        for f in range(2):
                            for k in range(DT):
                                last = nc.tensor.matmul(bank[2 * half + n][:, f * T:(f + 1) * T],
                                                        w[:, k, f * P:(f + 1) * P], h[:, k, :],
                                                        start=(k == 0), stop=(k == DT - 1))
                        last.then_inc(chunk_done, 1)

                def down_half(j, half, turns, done, final=False):
                    pe.wait_ge(hid_done, done)
                    accumulate(c0 + j, [hid[:, 2 * half + k, :] for k in range(2)], turns, final)

                for tt in range(TT):
                    for k in range(DT):
                        last = nc.tensor.matmul(bank[3][:, tt * NE:(tt + 1) * NE],
                                                h[:, k, tt * P:(tt + 1) * P], router[:, k, :],
                                                start=(k == 0), stop=(k == DT - 1))
                last.then_inc(logits, 1)
                zero_acc()
                up_half(0, 0, 0, None)
                pe.wait_ge(gates_ready, layer + 1)
                for tt in range(TT):
                    last = nc.tensor.transpose(bank[3][0:NE, tt * P:(tt + 1) * P],
                                               gates[:, tt, :], ident)
                last.then_inc(gates_t, 1)
                pe.wait_ge(gates_copied, layer + 1)
                if layer == 0:
                    pe.wait_ge(two_loaded, 10 * 16)
                for e in range(NE):
                    n = e // 2
                    if e % 2 == 0 and n >= 2:
                        pe.wait_ge(gb_done, layer * 8 + n - 1)
                    last = nc.tensor.matmul(bank[2 + n % 2][:, e % 2 * T:e % 2 * T + T],
                                            pick[0:NE, e * P:(e + 1) * P], gate_t[:, :],
                                            start=True, stop=True)
                    if e % 2 == 1:
                        last.then_inc(gb_ready, 1)
                pe.wait_ge(gb_done, layer * 8 + 8)
                up_half(2, 1, 0, None)
                down_half(4, 0, 0, halves + 1)
                with pe.Fori(1, NE) as e:
                    up_half(5, 0, e - 1, halves + 2 * e - 1)
                    down_half(7, 1, e - 1, halves + 2 * e)
                    up_half(8, 1, e - 1, None)
                    down_half(10, 0, e - 1, halves + 2 * e + 1)
                down_half(6 * NE - 1, 1, 0, halves + 2 * NE, final=True)

            layer_norm("mix0")
            experts(0)
            layer_norm("ffn0")
            for j in range(4):
                project("k2", j, h)
            for j in range(4):
                project_rows("v2", j, h)
            for j in range(4):
                project("q2", j, h)
            for unit in range(U0["w_o"] - 3, U0["w_o"]):
                evacuated(pe, unit)
            n1 = len(tiles)

            def scores2(i):
                hd, qt = tiles[i]
                if i >= 2:
                    pe.wait_ge(s_read, n1 + i - 1)
                row, n = hd % 2 * HD, (qt + 1) * P
                for c in range(2):
                    ft = c * 4 + hd // 2
                    last = nc.tensor.matmul(bank[3 + i % 2][:, c * T:c * T + n],
                                            q2[row:row + HD, ft, qt * P:(qt + 1) * P],
                                            k2[row:row + HD, ft, 0:n], start=True, stop=True)
                last.then_inc(s_ready, 1)

            def transposes2(i):
                pe.wait_ge(p_ready, n1 + i + 1)
                if i >= 2:
                    pe.wait_ge(o_done, n1 + i - 1)
                for kt in range(tiles[i][1] + 1):
                    last = nc.tensor.transpose(bank[5 + i % 2][:, kt * P:(kt + 1) * P],
                                               pr2[:, i % 2, 0, kt * P:(kt + 1) * P], ident)
                last.then_inc(t_ready, 1)

            def values2(i):
                hd, qt = tiles[i]
                pe.wait_ge(pt_ready, n1 + i + 1)
                for kt in range(qt + 1):
                    last = nc.tensor.matmul(bank[5 + i % 2][:, T:T + P],
                                            pt2[:, i % 2, kt * P:(kt + 1) * P],
                                            v2[:, kt, hd * P:(hd + 1) * P],
                                            start=(kt == 0), stop=(kt == qt))
                last.then_inc(pv_done, 1)

            scores2(0)
            for i in range(n1):
                if i + 1 < n1:
                    scores2(i + 1)
                if i >= 1:
                    values2(i - 1)
                transposes2(i)
            values2(n1 - 1)
            pe.wait_ge(sub_scaled, 1)
            for hd in range(HEADS):
                for qt in range(TT):
                    last = nc.tensor.transpose(bank[hd // 2][:, hd % 2 * T + qt * P:hd % 2 * T + qt * P + P],
                                               o_rows(qt)[:, hd * P:(hd + 1) * P], ident)
                if hd % 2 == 1:
                    last.then_inc(sub_t, 1)
            pe.wait_ge(sub_out, 4)
            for j in range(4):
                project("w_o", j, at_out)
            layer_norm("mix1")
            experts(1)
            layer_norm("ffn1")

        @block.scalar
        def _(sc):
            step = [0]

            def own(ins):
                step[0] += 1
                ins.then_inc(act_step, 1)
                sc.wait_ge(act_step, step[0])

            act_ = nc.scalar.activation

            def square(src, dst):
                act_(dst, src, ACT.Square).then_inc(stat_in, 1)

            def sqrt_mean(stat, e):
                sc.wait_ge(stat_out, stat)
                act_(root[:, :], bank[3][:, 0:T], ACT.Sqrt, bias=eps[:, e:e + 1])\
                    .then_inc(root_ready, 1)

            def free(ins, unit):
                ins.then_inc(unit_free[unit % UNIT_BANKS], 1)

            sc.wait_ge(x_loaded, 16)
            square(h[:, :, :], sq1)
            for hd in range(HEADS):
                sc.wait_ge(rows_ready, hd + 1)
                act_(rows[:, hd, :], bank[hd][:, 0:RELS], ACT.Copy).then_inc(rows_copied, 1)
            sc.wait_ge(set_up, 6)
            sqrt_mean(STATS["mix"], 0)
            sc.wait_ge(angles_ready, 1)
            act_(sin_t, ang, ACT.Sin).then_inc(rope_ready, 1)
            act_(cos_t, ang, ACT.Sin, scale=0.5).then_inc(rope_ready, 1)
            sc.wait_ge(norm_done, NORMS["mix"])
            for j in range(4):
                computed(sc, "c", j)
                free(act_(cgate[:, 2 * j:2 * j + 2, :], unit_bank(U0["c"] + j)[:, :], ACT.Copy),
                     U0["c"] + j)
            sc.wait_ge(rows_stored, 16)
            for j in range(12):
                computed(sc, "q", j)
                free(act_(qk[:, 2 * j:2 * j + 2, :], unit_bank(U0["q"] + j)[:, :], ACT.Copy),
                     U0["q"] + j)
            for j in range(6):
                computed(sc, "v", j)
                free(act_(v1[:, :, j * T:(j + 1) * T],
                          unit_bank(U0["v"] + j)[:, :].rearrange("p (a b) -> p a b", a=TT), ACT.Copy),
                     U0["v"] + j)
            for name, dst, b0 in (("gc", sig_c, 0), ("ga", sig_a, 8)):
                for j in range(4):
                    computed(sc, name, j)
                    for n in range(2):
                        ins = act_(dst[:, 2 * j + n, :], unit_bank(U0[name] + j)[:, n * T:(n + 1) * T],
                                   ACT.Sigmoid, bias=V("gate_bias", b0 + 2 * j + n))
                    free(ins, U0[name] + j)

            n1 = HEADS * TT

            def nblocks(i):
                return GROUPS * (i % 2 + 1)

            def exp1(i):
                n = (i % 2 + 1) * P
                sc.wait_ge(max_ready, i + 1)
                if i >= 2:
                    sc.wait_ge(t_ready, i - 1)
                act_(pr1[:, i % 2, :, 0:n], sc1[:, i % 2, :, 0:n], ACT.Exp,
                     bias=neg_max[:, i % 2:i % 2 + 1], accum_out=denom[:, i % 2:i % 2 + 1])\
                    .then_inc(exp_done, 1)

            def copy_t1(i):
                tb = [(0, 1), (2, 7)][i % 2]
                sc.wait_ge(t_ready, i + 1)
                if i >= 2:
                    sc.wait_ge(pv_done, i - 1)
                n = nblocks(i)
                ins = act_(pt1[:, i % 2, 0:min(n, 4) * P], bank[tb[0]][:, 0:min(n, 4) * P], ACT.Copy)
                if n > 4:
                    ins = act_(pt1[:, i % 2, 4 * P:n * P], bank[tb[1]][:, 0:(n - 4) * P], ACT.Copy)
                ins.then_inc(pt_ready, 1)

            def out1(i):
                hd, qt = i // 2, i % 2
                row = hd % 2 * HD
                sc.wait_ge(pv_done, i + 1)
                act_(o_t[row:row + HD, hd // 2, qt * P:(qt + 1) * P],
                     bank[[1, 7][i % 2]][row:row + HD, T:T + P], ACT.Copy).then_inc(o_done, 1)

            for i in range(n1 + 2):
                if i < n1:
                    exp1(i)
                if 1 <= i <= n1:
                    copy_t1(i - 1)
                if i >= 2:
                    out1(i - 2)

            sc.wait_ge(res_done, RES["mixer"])
            square(h[:, :, :], sq1)
            sqrt_mean(STATS["ffn"], 0)
            sc.wait_ge(norm_done, NORMS["ffn"])
            for j in range(8):
                computed(sc, "wq", j)
                free(act_(pq[:, 2 * j:2 * j + 2, :], unit_bank(U0["wq"] + j)[:, :], ACT.Copy),
                     U0["wq"] + j)
            for j in range(8):
                sc.wait_ge(key_s, j + 1)
                free(act_(score[:, j // 4, j % 4 * 4:j % 4 * 4 + 4, :],
                          unit_bank(U0["keyscore"] + j)[:, :], ACT.Copy), U0["keyscore"] + j)

            def gelu(j, turns=None):
                unit = U0["down"] + j
                if turns is None:
                    computed(sc, "down", j)
                    dst = act[:, 2 * j:2 * j + 2, :]
                else:
                    sc.wait_ge(chunk_done, C0["down"] + j + 1 + turns * 6)
                    dst = act[:, bass.ds(turns * 12 + 2 * j, 2), :]
                free(act_(dst, unit_bank(unit)[:, :].rearrange("p (a b) -> p a b", a=2), ACT.Gelu), unit)

            with sc.Fori(0, 4) as it:
                for j in range(6):
                    gelu(j, it)
            sc.wait_ge(best_ready, 1)
            for tt in range(TT):
                act_(best[:, tt], best[:, tt], ACT.Exp).then_inc(best_exp, 1)
            with sc.Fori(4, 6) as it:
                for j in range(6):
                    gelu(j, it)
            sc.wait_ge(slots_copied, 1)
            with sc.Fori(6, 10) as it:
                for j in range(6):
                    gelu(j, it)
            for j in range(60, 64):
                gelu(j)

            sc.wait_ge(res_done, RES["experts"])
            square(h[:, :, :], sq2)
            sqrt_mean(STATS["final"], 0)
            sc.wait_ge(norm_done, NORMS["final"])
            sc.wait_ge(lam_sum, 1)
            act_(lam[:, 0:2], lam[:, 2:4], ACT.Exp).then_inc(lam_exp, 1)
            for j in range(8):
                computed(sc, "pw1", j)
                if j >= 2:
                    evacuated(sc, U0["pw1"] + j - 2)
                act_(sg2[:, j % 2, :], unit_bank(U0["pw1"] + j)[:, T:HALF], ACT.Sigmoid,
                     bias=V("b_pw1", 8 + j)).then_inc(glu_sig, 1)

            def layer_norm(name, g, b, g0, dst, func=ACT.Identity):
                n = LNS[name]
                sc.wait_ge(centred, n)
                square(cen, sq2)
                sqrt_mean(STATS[name] + 1, 1)
                sc.wait_ge(scaled, n)
                for k in range(DT):
                    ins = act_(dst[:, k, :], nrm[:, k, :], func, bias=V(b, g0 + k),
                               scale=V(g, g0 + k))
                ins.then_inc(norm_done, 1)

            layer_norm("conv", "ln_g", "ln_b", 0, cen, ACT.Silu)
            for j in range(4):
                computed(sc, "pw2", j)
                for n in range(2):
                    ins = act_(sq2[:, 2 * j + n, :],
                               unit_bank(U0["pw2"] + j)[:, n * T:(n + 1) * T], ACT.Identity,
                               bias=V("b_pw2", 2 * j + n))
                free(ins, U0["pw2"] + j)

            def experts(layer):
                sc.wait_ge(logits, layer + 1)
                act_(aff, bank[3][:, 0:TT * NE], ACT.Sigmoid).then_inc(affin, 1)
                for n in range(8):
                    sc.wait_ge(gb_ready, layer * 8 + n + 1)
                    act_(gate_b[:, 2 * n:2 * n + 2, :], bank[2 + n % 2][:, :], ACT.Copy)\
                        .then_inc(gb_done, 1)
                c0, halves = C0[f"moe{layer}"], 2 * NE * layer

                def half_silu(half, chunk, done):
                    sc.wait_ge(chunk_done, chunk)
                    if done is not None:
                        sc.wait_ge(hid_done, done)
                    act_(silu[:, half, :], bank[2 * half][:, :], ACT.Silu).then_inc(silu_done, 1)

                half_silu(0, c0 + 1, None)
                half_silu(1, c0 + 3, None)
                with sc.Fori(1, NE) as e:
                    half_silu(0, e * 6 + c0, halves + 2 * e - 1)
                    half_silu(1, e * 6 + c0 + 3, halves + 2 * e)

            layer_norm("mix0", "ln_mix_g", "ln_mix_b", 0, h)
            experts(0)
            layer_norm("ffn0", "ln_ffn_g", "ln_ffn_b", 0, h)
            for name, dst in (("k2", k2), ("v2", None), ("q2", q2)):
                for j in range(4):
                    computed(sc, name, j)
                    if dst is None:
                        out, src = v2[:, :, j * T:(j + 1) * T], \
                            unit_bank(U0[name] + j)[:, :].rearrange("p (a b) -> p a b", a=TT)
                    else:
                        out, src = dst[:, 2 * j:2 * j + 2, :], unit_bank(U0[name] + j)[:, :]
                    free(act_(out, src, ACT.Copy), U0[name] + j)

            def exp2(i):
                n = (i % 2 + 1) * P
                sc.wait_ge(max_ready, n1 + i + 1)
                if i >= 2:
                    sc.wait_ge(t_ready, n1 + i - 1)
                for c in range(2):
                    ins = act_(pr2[:, i % 2, c, 0:n], sc2[:, i % 2, c, 0:n], ACT.Exp,
                               bias=neg_max[:, i % 2 * 2 + c:i % 2 * 2 + c + 1],
                               accum_out=denom[:, i % 2 * 2 + c:i % 2 * 2 + c + 1])
                ins.then_inc(exp_done, 1)

            def copy_t2(i):
                n = (i % 2 + 1) * P
                sc.wait_ge(t_ready, n1 + i + 1)
                if i >= 2:
                    sc.wait_ge(pv_done, n1 + i - 1)
                act_(pt2[:, i % 2, 0:n], bank[5 + i % 2][:, 0:n], ACT.Copy).then_inc(pt_ready, 1)

            def out2(i):
                hd, qt = i // 2, i % 2
                sc.wait_ge(pv_done, n1 + i + 1)
                src = bank[5 + i % 2][:, T:T + P]
                own(act_(sq2[:, i % 2, 0:P], src, ACT.Square,
                         accum_out=sumsq[:, i:i + 1]))
                act_(o_rows(qt)[:, hd * P:(hd + 1) * P], src, ACT.Copy).then_inc(o_done, 1)

            for i in range(n1 + 2):
                if i < n1:
                    exp2(i)
                if 1 <= i <= n1:
                    copy_t2(i - 1)
                if i >= 2:
                    out2(i - 2)
            sc.wait_ge(o_done, 2 * n1)
            act_(sumsq, sumsq, ACT.Sqrt, bias=eps[:, 1:2], scale=1.0 / P).then_inc(sub_root, 1)
            for n in range(4):
                sc.wait_ge(sub_t, n + 1)
                act_(at_out[:, 2 * n:2 * n + 2, :], bank[n][:, :], ACT.Copy,
                     scale=sub_g).then_inc(sub_out, 1)
            layer_norm("mix1", "ln_mix_g", "ln_mix_b", 8, h)
            experts(1)
            layer_norm("ffn1", "ln_ffn_g", "ln_ffn_b", 8, h)

        @block.vector
        def _(ve):
            step = [0]
            vx = nc.vector

            def own(ins):
                step[0] += 1
                ins.then_inc(dve_step, 1)
                ve.wait_ge(dve_step, step[0])

            def free(ins, unit):
                ins.then_inc(unit_free[unit % UNIT_BANKS], 1)

            def pair(ap):
                return ap.rearrange("p (a b) -> p a b", a=2)

            def rms_apply(name, vname, dst):
                ve.wait_ge(root_ready, ROOTS[name])
                own(vx.reciprocal(root[:, :], root[:, :]))
                for k in range(DT):
                    ins = vx.scalar_tensor_tensor(dst[:, k, :], h[:, k, :], V(vname, k), root[:, :],
                                                  ALU.mult, ALU.mult)
                ins.then_inc(norm_done, 1)

            ve.wait_ge(loaded, 9 * 16)
            own(vx.tensor_copy(turn, ang.bitcast(I32)))
            own(vx.tensor_scalar(ang, turn, C("freq"), None, ALU.mult))
            magic = 1.5 * 2.0 ** 23
            own(vx.tensor_scalar(turn, ang, 1.0 / (2 * math.pi), magic, ALU.mult, ALU.add))
            own(vx.tensor_scalar(turn, turn, magic, None, ALU.subtract))
            c1 = 6.28125
            c2 = float(np.float32(np.round((2 * math.pi - c1) * 2 ** 20) / 2 ** 20))
            c3 = 2 * math.pi - c1 - c2
            for c in (c1, c2, c3):
                own(vx.scalar_tensor_tensor(ang, turn, -c, ang, ALU.mult, ALU.add))
            vx.tensor_scalar(ang, ang, 3.1415925, -3.1415925, ALU.min, ALU.max)\
                .then_inc(angles_ready, 1)
            ve.wait_ge(rope_ready, 2)
            own(vx.tensor_tensor(cos_t, cos_t, cos_t, ALU.mult))
            own(vx.tensor_scalar(cos_t, cos_t, -2.0, 1.0, ALU.mult, ALU.add))
            rms_apply("mix", "norm_mix", u)

            ve.wait_ge(set_up, 6)
            for j in range(4):
                computed(ve, "xc", j)
                evacuated(ve, U0["c"] + j)
                free(vx.tensor_tensor(z[:, 2 * j:2 * j + 2, 2:T + 2], cgate[:, 2 * j:2 * j + 2, :],
                                      pair(unit_bank(U0["xc"] + j)[:, :]), ALU.mult), U0["xc"] + j)
            for j in range(4):
                evacuated(ve, U0["xc"] + j)
            for i in range(3):
                for k in range(DT):
                    src = z[:, k, i:i + T]
                    if i == 0:
                        ins = vx.tensor_scalar(conv[:, k, :], src, V("conv_w", k), None, ALU.mult)
                    else:
                        ins = vx.scalar_tensor_tensor(conv[:, k, :], src, V("conv_w", i * 8 + k),
                                                      conv[:, k, :], ALU.mult, ALU.add)
                own(ins)
            for j in range(4):
                computed(ve, "b", j)
                free(vx.tensor_tensor(conv[:, 2 * j:2 * j + 2, :], conv[:, 2 * j:2 * j + 2, :],
                                      pair(unit_bank(U0["b"] + j)[:, :]), ALU.mult), U0["b"] + j)
            for j in range(12):
                ve.wait_ge(rot_ready, j + 1)
                t = qk[:, 2 * j:2 * j + 2, :]
                vx.tensor_tensor(rot_tmp, pair(bank[3 + j % 2][:, :]),
                                 sin_t.unsqueeze(1).broadcast_to([P, 2, T]), ALU.mult)
                own(vx.tensor_tensor(t, t, cos_t.unsqueeze(1).broadcast_to([P, 2, T]), ALU.mult))
                vx.tensor_tensor(t, t, rot_tmp, ALU.add).then_inc(rot_done, 1)
                ve.wait_ge(rot_done, j + 1)
            for j in range(4):
                computed(ve, "conv_out", j)
                evacuated(ve, U0["gc"] + j)
                free(vx.tensor_tensor(merged[:, 2 * j:2 * j + 2, :], sig_c[:, 2 * j:2 * j + 2, :],
                                      pair(unit_bank(U0["conv_out"] + j)[:, :]), ALU.mult),
                     U0["conv_out"] + j)

            n1 = HEADS * TT

            def masked(i):
                qt, s = i % 2, i % 2
                n = (qt + 1) * P
                ve.wait_ge(s_ready, i + 1)
                if i >= 2:
                    ve.wait_ge(exp_done, i - 1)
                b0, b1 = bank[3 + s * 2], bank[4 + s * 2]
                vx.scalar_tensor_tensor(sc1[:, s, 0:2, 0:n], pair(b0[:, :])[:, :, 0:n], HD ** -0.5,
                                        mask[:, 0:2, (1 - qt) * P:(1 - qt) * P + n],
                                        ALU.mult, ALU.add)
                vx.scalar_tensor_tensor(sc1[:, s, 2, 0:n], b1[:, 0:n], HD ** -0.5,
                                        mask[:, 2, (1 - qt) * P:(1 - qt) * P + n],
                                        ALU.mult, ALU.add).then_inc(s_read, 1)
                ve.wait_ge(s_read, i + 1)
                vx.tensor_reduce(neg_max[:, s:s + 1], sc1[:, s, :, 0:n], AX.XY, ALU.max,
                                 negate=True).then_inc(max_ready, 1)

            def normal(i):
                s, n = i % 2, (i % 2 + 1) * P
                ve.wait_ge(exp_done, i + 1)
                own(vx.reciprocal(rden[:, s:s + 1], denom[:, s:s + 1]))
                vx.tensor_scalar(pr1[:, s, :, 0:n], pr1[:, s, :, 0:n], rden[:, s:s + 1], None,
                                 ALU.mult).then_inc(p_ready, 1)

            masked(0)
            for i in range(n1):
                if i + 1 < n1:
                    masked(i + 1)
                normal(i)

            for j in range(4):
                computed(ve, "attn_out", j)
                evacuated(ve, U0["ga"] + j)
                src = pair(unit_bank(U0["attn_out"] + j)[:, :])
                m = merged[:, 2 * j:2 * j + 2, :]
                own(vx.tensor_tensor(rot_tmp, sig_a[:, 2 * j:2 * j + 2, :], src, ALU.mult))
                free(vx.tensor_tensor(m, m, rot_tmp, ALU.add), U0["attn_out"] + j)
                evacuated(ve, U0["attn_out"] + j)
            for j in range(4):
                computed(ve, "w_out", j)
                hh = h[:, 2 * j:2 * j + 2, :]
                free(vx.tensor_tensor(hh, hh, pair(unit_bank(U0["w_out"] + j)[:, :]), ALU.add),
                     U0["w_out"] + j)
            own(vx.memset(neg_max, 0.0))
            vx.memset(denom, 0.0).then_inc(res_done, 1)
            rms_apply("ffn", "norm_ffn", u)

            for j in range(8):
                evacuated(ve, U0["keyscore"] + j)
            both = [(tt, c) for tt in range(TT) for c in range(2 * PH)]
            ti = top_i.bitcast(U32)
            for tt, c in both:
                ins = vx.max(top_v[:, tt, c, 0:8], score[:, tt, c, :])
            own(ins)
            for tt, c in both:
                ins = vx.max_index(ti[:, tt, c, 0:8], top_v[:, tt, c, 0:8], score[:, tt, c, :])
            own(ins)
            for tt, c in both:
                ins = vx.match_replace(score[:, tt, c, :], top_v[:, tt, c, 0:8], score[:, tt, c, :], -3e38)
            own(ins)
            for tt, c in both:
                ins = vx.max(top_v[:, tt, c, 8:16], score[:, tt, c, :])
            own(ins)
            for tt, c in both:
                ins = vx.max_index(ti[:, tt, c, 8:16], top_v[:, tt, c, 8:16], score[:, tt, c, :])
            own(ins)
            own(vx.tensor_copy(top_f, ti))
            bi = best_i.bitcast(U32)
            for tt in range(TT):
                for hd in range(PH):
                    ins = vx.tensor_tensor(
                        cand[:, hd, :].rearrange("p (a b) -> p a b", a=TOPK),
                        top_v[:, tt, 2 * hd, :].unsqueeze(2).broadcast_to([P, TOPK, TOPK]),
                        top_v[:, tt, 2 * hd + 1, :].unsqueeze(1).broadcast_to([P, TOPK, TOPK]), ALU.add)
                own(ins)
                for hd in range(PH):
                    ins = vx.max(best[:, tt, hd, 0:8], cand[:, hd, :])
                own(ins)
                for hd in range(PH):
                    ins = vx.max_index(bi[:, tt, hd, 0:8], best[:, tt, hd, 0:8], cand[:, hd, :])
                own(ins)
                for hd in range(PH):
                    ins = vx.match_replace(cand[:, hd, :], best[:, tt, hd, 0:8], cand[:, hd, :], -3e38)
                own(ins)
                for hd in range(PH):
                    ins = vx.max(best[:, tt, hd, 8:16], cand[:, hd, :])
                own(ins)
                for hd in range(PH):
                    ins = vx.max_index(bi[:, tt, hd, 8:16], best[:, tt, hd, 8:16], cand[:, hd, :])
                own(ins)
            for tt in range(TT):
                own(vx.tensor_copy(slot[:, 2, tt, 0:PH], best[:, tt, :, 0]))
                ins = vx.tensor_tensor(best[:, tt], best[:, tt],
                                       slot[:, 2, tt, 0:PH].unsqueeze(2).broadcast_to([P, PH, TOPK]),
                                       ALU.subtract)
                if tt == 0:
                    own(ins)
            ins.then_inc(best_ready, 1)
            bi_flat = bi.rearrange("p a b c -> p a (b c)")
            pa, pb = pos_a.bitcast(U32), pos_b.bitcast(U32)
            vx.tensor_scalar(pa, bi_flat, 4, None, ALU.logical_shift_right)
            own(vx.tensor_scalar(pb, bi_flat, TOPK - 1, None, ALU.bitwise_and))
            vx.tensor_copy(pos_f[:, 0], pa)
            own(vx.tensor_copy(pos_f[:, 1], pb))
            iota = C("iota")[:, 0:TOPK]
            for tt in range(TT):
                for half in range(2):
                    for hd in range(PH):
                        ins = vx.tensor_tensor(
                            match[:, hd],
                            pos_f[:, half, tt, hd * TOPK:(hd + 1) * TOPK].unsqueeze(2)
                            .broadcast_to([P, TOPK, TOPK]),
                            iota.unsqueeze(1).broadcast_to([P, TOPK, TOPK]), ALU.is_equal)
                    own(ins)
                    for hd in range(PH):
                        ins = vx.tensor_tensor(
                            match[:, hd], match[:, hd],
                            top_f[:, tt, 2 * hd + half, :].unsqueeze(1).broadcast_to([P, TOPK, TOPK]),
                            ALU.mult)
                    own(ins)
                    own(vx.tensor_reduce(slot[:, half, tt, :].rearrange("p (a b) -> p a b", a=PH),
                                         match, AX.X, ALU.add))
            for tt in range(TT):
                ve.wait_ge(best_exp, tt + 1)
                own(vx.tensor_reduce(gsum[:, tt, :], best[:, tt], AX.X, ALU.add))
                own(vx.reciprocal(gsum[:, tt, :], gsum[:, tt, :]))
                ins = vx.tensor_tensor(slot[:, 2, tt, :].rearrange("p (a b) -> p a b", a=PH), best[:, tt],
                                       gsum[:, tt, :].unsqueeze(2).broadcast_to([P, PH, TOPK]), ALU.mult)
                if tt == 0:
                    own(ins)
            ins.then_inc(slots_ready, 1)
            ve.wait_ge(slots_t, 1)
            for n in range(3):
                vx.tensor_copy(slot_t[:, n, :], bank[4 + n][:, 0:T])\
                    .then_inc([gated[0], gated[1], slots_copied][n], 1)
            computed(ve, "down", 63)
            ve.wait_ge(slots_copied, 1)
            for unit in range(U0["pw1"] - 3, U0["pw1"]):
                evacuated(ve, unit)
            with ve.Fori(0, T // 8) as it:
                for half in range(2):
                    ve.wait_ge(scattered[half], it + 1)
                    for tk in range(4):
                        a = u[:, half * 4 + tk // 2, tk % 2 * P:tk % 2 * P + P]
                        b = u[:, half * 4 + 2 + tk // 2, tk % 2 * P:tk % 2 * P + P]
                        at = it * 8 + (half * 4 + tk)
                        vx.tensor_scalar(a, C("iota"), slot_t[:, 0, bass.ds(at, 1)], None, ALU.is_equal)
                        ins = vx.tensor_scalar(b, C("iota"), slot_t[:, 1, bass.ds(at, 1)],
                                               slot_t[:, 2, bass.ds(at, 1)], ALU.is_equal, ALU.mult)
                    ins.then_inc(onehot_ready[half], 1)
                for half in range(2):
                    ve.wait_ge(scattered[half], it + 2)
                    a = act[:, :, bass.ds(it * 8 + half * 4, 4)]
                    vx.tensor_tensor(a, a, bank[4 + half][:, :].rearrange("p (i t) -> p i t", t=4),
                                     ALU.mult).then_inc(gated[half], 1)

            def residual(done, scale):
                for b_ in range(4):
                    hh = h[:, 2 * b_:2 * b_ + 2, :]
                    if scale is None:
                        ins = vx.tensor_tensor(hh, hh, pair(bank[4 + b_][:, :]), ALU.add)
                    else:
                        ins = vx.scalar_tensor_tensor(pre[:, 2 * b_:2 * b_ + 2, :], hh, scale,
                                                      pair(bank[4 + b_][:, :]), ALU.mult, ALU.add)
                return ins

            computed(ve, "up", 63)
            for half in range(2):
                ve.wait_ge(gated[half], T // 8 + 1)
            residual(None, None).then_inc(res_done, 1)
            rms_apply("final", "final_norm", h)

            ve.wait_ge(two_loaded, 10 * 16)
            own(vx.tensor_tensor(lamp[:, 1, 0:HD], lamp[:, 0, 0:HD], lamp[:, 0, HD:2 * HD], ALU.mult))
            own(vx.tensor_tensor(lamp[:, 1, HD:2 * HD], lamp[:, 0, 2 * HD:3 * HD],
                                 lamp[:, 0, 3 * HD:4 * HD], ALU.mult))
            vx.tensor_reduce(lam[:, 2:4], lamp[:, 1, 0:2 * HD].rearrange("p (a b) -> p a b", a=2),
                             AX.X, ALU.add).then_inc(lam_sum, 1)
            ve.wait_ge(lam_exp, 1)
            own(vx.tensor_tensor(lam[:, 2:3], lam[:, 1:2], lam[:, 0:1], ALU.subtract))
            own(vx.tensor_scalar(lam[:, 2:3], lam[:, 2:3], LAMBDA_INIT, None, ALU.subtract))
            own(vx.tensor_scalar(sub_g, V("subln_g", 0), 1.0 - LAMBDA_INIT, None, ALU.mult))
            own(vx.memset(glu[:, :, 0:TAPS - 1], 0.0))
            for j in range(8):
                ve.wait_ge(glu_sig, j + 1)
                free(vx.scalar_tensor_tensor(glu[:, j, TAPS - 1:TAPS - 1 + T],
                                             unit_bank(U0["pw1"] + j)[:, 0:T], V("b_pw1", j),
                                             sg2[:, j % 2, :], ALU.add, ALU.mult), U0["pw1"] + j)
                if j % 2 == 0:
                    continue
                evacuated(ve, U0["pw1"] + j - 1)
                evacuated(ve, U0["pw1"] + j)
                for k in (j - 1, j):
                    step[0] += 1
                    vx.tensor_scalar(pre[:, k, :], glu[:, k, 0:T], V("w_dw", k), V("b_dw", k),
                                     ALU.mult, ALU.add).then_inc(dve_step, 1)
                for i in range(1, TAPS):
                    for k in (j - 1, j):
                        step[0] += 1
                        ve.wait_ge(dve_step, step[0] - 2)
                        vx.scalar_tensor_tensor(pre[:, k, :], glu[:, k, i:i + T], V("w_dw", i * 8 + k),
                                                pre[:, k, :], ALU.mult, ALU.add).then_inc(dve_step, 1)
            ve.wait_ge(dve_step, step[0])
            own(vx.memset(mx8, 0.0))
            vx.memset(mx8, 0.0).then_inc(stat_in, 1)

            def layer_norm(name):
                ve.wait_ge(stat_out, STATS[name])
                vx.tensor_tensor(cen, pre, bank[3][:, 0:T].unsqueeze(1).broadcast_to([P, DT, T]),
                                 ALU.subtract).then_inc(centred, 1)
                ve.wait_ge(root_ready, ROOTS[name])
                own(vx.reciprocal(root[:, :], root[:, :]))
                vx.tensor_tensor(nrm, cen, root[:, :].unsqueeze(1).broadcast_to([P, DT, T]),
                                 ALU.mult).then_inc(scaled, 1)

            layer_norm("conv")
            for j in range(4):
                evacuated(ve, U0["pw2"] + j)
                ins = vx.scalar_tensor_tensor(pre[:, 2 * j:2 * j + 2, :], h[:, 2 * j:2 * j + 2, :], ALPHA,
                                              sq2[:, 2 * j:2 * j + 2, :], ALU.mult, ALU.add)
            ins.then_inc(stat_in, 1)
            layer_norm("mix0")

            def experts(layer):
                ve.wait_ge(affin, layer + 1)
                own(vx.tensor_tensor(sel, aff, rbias[:, :].unsqueeze(1).broadcast_to([P, TT, NE]), ALU.add))
                low = C("lower").rearrange("p (a b) -> p a b", a=EPG)
                big4 = prod.rearrange("p a b -> p (a b)")[:, 0:128]
                big4b = prod.rearrange("p a b -> p (a b)")[:, 128:256]

                def ranks(values, out, n):
                    v4 = values.rearrange("p (n e) -> p n e", e=EPG)
                    for g in range(n):
                        other = v4[:, g, :].unsqueeze(1).broadcast_to([P, EPG, EPG])
                        mine = v4[:, g, :].unsqueeze(2).broadcast_to([P, EPG, EPG])
                        a = big4[:, g * 16:(g + 1) * 16].rearrange("p (a b) -> p a b", a=EPG)
                        b = big4b[:, g * 16:(g + 1) * 16].rearrange("p (a b) -> p a b", a=EPG)
                        vx.tensor_tensor(a, other, mine, ALU.is_gt)
                        ins = vx.tensor_tensor(b, other, mine, ALU.is_equal)
                    own(ins)
                    m = n * 16
                    bb = big4b[:, 0:m].rearrange("p (n m) -> p n m", m=16)
                    own(vx.tensor_tensor(bb, bb, C("lower").unsqueeze(1).broadcast_to([P, n, 16]), ALU.mult))
                    own(vx.tensor_tensor(big4[:, 0:m], big4[:, 0:m], big4b[:, 0:m], ALU.add))
                    own(vx.tensor_reduce(out, big4[:, 0:m].rearrange("p (n m) -> p n m", m=EPG),
                                         AX.X, ALU.add))

                sel_f = sel.rearrange("p a b -> p (a b)")
                top2_f = top2.rearrange("p a b -> p (a b)")
                gsel_f = gsel.rearrange("p a b -> p (a b)")
                ranks(sel_f, rank, TT * NG)
                own(vx.tensor_scalar(top2_f, rank, 1.5, None, ALU.is_lt))
                own(vx.tensor_tensor(gsel_f, sel_f, top2_f, ALU.mult))
                own(vx.tensor_reduce(gscore, gsel_f.rearrange("p (n e) -> p n e", e=EPG), AX.X, ALU.add))
                ranks(gscore, grank, TT)
                own(vx.tensor_scalar(grank, grank, 0.5, None, ALU.is_lt))
                own(vx.tensor_tensor(top2_f.rearrange("p (n e) -> p n e", e=EPG),
                                     top2_f.rearrange("p (n e) -> p n e", e=EPG),
                                     grank.unsqueeze(2).broadcast_to([P, TT * NG, EPG]), ALU.mult))
                own(vx.tensor_tensor(gates, aff, top2, ALU.mult))
                own(vx.tensor_reduce(wsum, gates, AX.X, ALU.add))
                own(vx.reciprocal(wsum, wsum))
                vx.tensor_tensor(gates, gates, wsum.unsqueeze(2).broadcast_to([P, TT, NE]), ALU.mult)\
                    .then_inc(gates_ready, 1)
                ve.wait_ge(gates_t, layer + 1)
                vx.tensor_copy(gate_t[:, :], bank[3][0:NE, 0:T]).then_inc(gates_copied, 1)
                ve.wait_ge(gb_done, layer * 8 + 8)
                c0, halves = C0[f"moe{layer}"], 2 * NE * layer

                def hidden(half, e, chunk, down, silus):
                    ve.wait_ge(chunk_done, chunk)
                    ve.wait_ge(silu_done, silus)
                    if down is not None:
                        ve.wait_ge(chunk_done, down)
                    pr = prod
                    if not (isinstance(silus, int) and silus == 1):
                        ve.wait_ge(hid_done, silus - 1)
                    vx.tensor_tensor(pr, pair(silu[:, half, :]), pair(bank[2 * half + 1][:, :]),
                                     ALU.mult).then_inc(mix_b, 1)
                    ve.wait_ge(mix_b, silus)
                    gb = gate_b[:, e, :] if isinstance(e, int) else gate_b[:, bass.ds(e, 1), :].squeeze(1)
                    vx.tensor_tensor(hid[:, 2 * half:2 * half + 2, :], pr,
                                     gb.unsqueeze(1).broadcast_to([P, 2, T]), ALU.mult)\
                        .then_inc(hid_done, 1)

                hidden(0, 0, c0 + 2, None, halves + 1)
                hidden(1, 0, c0 + 4, None, halves + 2)
                with ve.Fori(1, NE) as e:
                    hidden(0, e, e * 6 + c0 + 1, e * 6 + c0 - 1, e * 2 + halves + 1)
                    hidden(1, e, e * 6 + c0 + 4, e * 6 + c0 + 2, e * 2 + halves + 2)
                ve.wait_ge(chunk_done, c0 + 6 * NE)
                residual(None, ALPHA).then_inc(stat_in, 1)

            experts(0)
            layer_norm("ffn0")

            def biased(i):
                hd, qt, s = i // 2, i % 2, i % 2
                n = (qt + 1) * P
                ve.wait_ge(s_ready, n1 + i + 1)
                if i >= 2:
                    ve.wait_ge(exp_done, n1 + i - 1)
                rel = relb[:, hd, (1 - qt) * P:(1 - qt) * P + n]
                vx.scalar_tensor_tensor(sc2[:, s, :, 0:n], pair(bank[3 + s][:, :])[:, :, 0:n], HD ** -0.5,
                                        rel.unsqueeze(1).broadcast_to([P, 2, n]), ALU.mult, ALU.add)\
                    .then_inc(s_read, 1)
                ve.wait_ge(s_read, n1 + i + 1)
                vx.tensor_reduce(neg_max[:, 2 * s:2 * s + 2], sc2[:, s, :, 0:n], AX.X, ALU.max,
                                 negate=True).then_inc(max_ready, 1)

            def difference(i):
                s, n = i % 2, (i % 2 + 1) * P
                ve.wait_ge(exp_done, n1 + i + 1)
                r = rden[:, 2 * s:2 * s + 2]
                own(vx.reciprocal(r, denom[:, 2 * s:2 * s + 2]))
                own(vx.tensor_tensor(r[:, 1:2], r[:, 1:2], lam[:, 2:3], ALU.mult))
                own(vx.tensor_scalar(pr2[:, s, 0, 0:n], pr2[:, s, 0, 0:n], r[:, 0:1], None, ALU.mult))
                vx.scalar_tensor_tensor(pr2[:, s, 0, 0:n], pr2[:, s, 1, 0:n], r[:, 1:2],
                                        pr2[:, s, 0, 0:n], ALU.mult, ALU.add).then_inc(p_ready, 1)

            biased(0)
            for i in range(n1):
                if i + 1 < n1:
                    biased(i + 1)
                difference(i)
            ve.wait_ge(sub_root, 1)
            own(vx.reciprocal(sumsq, sumsq))
            for qt in range(TT):
                o = o_rows(qt).rearrange("p (a b) -> p a b", a=HEADS)
                r = sumsq.rearrange("p (a b) -> p b a", b=TT)[:, qt, :]
                ins = vx.tensor_tensor(o, o, r.unsqueeze(2).broadcast_to([P, HEADS, P]), ALU.mult)
            ins.then_inc(sub_scaled, 1)
            for j in range(4):
                computed(ve, "w_o", j)
                ins = vx.scalar_tensor_tensor(pre[:, 2 * j:2 * j + 2, :], h[:, 2 * j:2 * j + 2, :], ALPHA,
                                              pair(unit_bank(U0["w_o"] + j)[:, :]), ALU.mult, ALU.add)
                if j < 3:
                    free(ins, U0["w_o"] + j)
            ins.then_inc(stat_in, 1)
            layer_norm("mix1")
            experts(1)
            layer_norm("ffn1")


def columns(w):
    k, n = w.shape
    c = w.reshape(k // P, P, n // 256, 256).transpose(2, 1, 0, 3).reshape(n // 256, P, k // P * 256)
    if c.shape[2] == CW:
        return c
    full = np.zeros((c.shape[0], P, CW), np.float32)
    full[:, :, 0:c.shape[2]] = c
    return full


def rows_of(w):
    return w.reshape(w.shape[0] // 256, 2, P, D).transpose(0, 2, 1, 3).reshape(-1, P, CW)


def stream(a):
    win = columns(a["w_in"][0])
    conv_in = [win[4:8], win[8:12], win[0:4]]
    parts = conv_in + [win[12:30], win[30:38], columns(a["w_conv_out"][0]),
                       columns(a["w_attn_out"][0]), columns(a["w_out"][0]),
                       columns(a["peer_w_query"][0]), columns(a["peer_down"][0].T),
                       rows_of(a["peer_up"][0])]
    pw1 = a["a_w_pw1_2"][0].reshape(D, 2, DT, P).transpose(0, 2, 1, 3).reshape(D, 2 * D)
    parts += [columns(pw1), columns(a["a_w_pw2_2"][0])]

    def moe(layer):
        out = []
        for e in range(NE):
            g = columns(a["moe_w_gate_2"][layer, e])
            u_ = columns(a["moe_w_up_2"][layer, e])
            d = rows_of(a["moe_w_down_2"][layer, e])
            out += [g[0:1], u_[0:1]] + ([prev] if e else []) + [g[1:2], u_[1:2], d[0:1]]
            prev = d[1:2]
        return out + [prev]

    kv = columns(a["w_kv_2"])
    parts += moe(0) + [kv, columns(a["b_w_q_2"][0]), columns(a["b_w_o_2"][0])] + moe(1)
    out = np.concatenate(parts)
    assert out.shape == (CHUNKS, P, CW), out.shape
    return out


def vectors(a):
    names = [a["norm_mix"], a["conv_w"], a["gate_bias"], a["norm_ffn"], a["final_norm"],
             a["a_b_pw1_2"], a["a_w_dw_2"], a["a_b_dw_2"], a["a_ln_g_2"], a["a_ln_b_2"],
             a["a_b_pw2_2"], a["ln_mix_g_2"], a["ln_mix_b_2"], a["ln_ffn_g_2"], a["ln_ffn_b_2"],
             a["b_subln_g_2"]]
    return np.ascontiguousarray(np.concatenate([v.reshape(-1, P) for v in names]).T)


def kernel(**inputs):
    import concourse.bacc as bacc
    from concourse.bass_utils import run_bass_kernel_spmd

    a = {k: np.asarray(v) for k, v in inputs.items()}
    c = constants()
    arrays = {
        "x": np.ascontiguousarray(a["x"][0].T.reshape(DT, P, T).transpose(1, 0, 2)),
        "weights": stream(a), "vectors": vectors(a), "consts": c["consts"], "mask": c["mask"],
        "onehot": c["onehot"], "pick": c["pick"], "positions": a["positions"].reshape(T),
        "keys": np.ascontiguousarray(a["peer_sub_keys"][0].reshape(2 * PH, NK, P).transpose(2, 0, 1)),
        "router": np.ascontiguousarray(a["router_w_2"].reshape(DT, P, NE).transpose(1, 0, 2)),
        "rbias": a["router_bias_2"], "lam": a["b_lambda_2"].reshape(-1), "rel": a["rel_bias_2"],
    }
    nc = bacc.Bacc("TRN2", target_bir_lowering=False, num_devices=1)
    args = [nc.dram_tensor(f"in_{n}", v.shape, mybir.dt.from_np(v.dtype), kind="ExternalInput").ap()
            for n, v in arrays.items()]
    rows = nc.dram_tensor("bias_rows", (HEADS, P, RELS), F32, kind="Internal").ap()
    out = nc.dram_tensor("out", (P, DT, T), F32, kind="ExternalOutput").ap()
    build(nc, *args, rows, out)
    r = run_bass_kernel_spmd(nc, [{f"in_{n}": v for n, v in arrays.items()}], core_ids=[0])
    got = r.results[0]["out"]
    return got.transpose(1, 0, 2).reshape(D, T).T.reshape(1, T, D)
```

```python
import math
from contextlib import ExitStack

import concourse.bass as bass
import numpy as np
from concourse import mybir
from concourse.alu_op_type import AluOpType as ALU

F32 = mybir.dt.float32
F32R = mybir.dt.float32r
BF16 = mybir.dt.bfloat16
I32 = mybir.dt.int32
U32 = mybir.dt.uint32
ACT = mybir.ActivationFunctionType
AX = mybir.AxisListType

P = 128
T = 256
D = 1024
DT = D // P
TT = T // P
HALF = 2 * T

HEADS = 8
GROUPS = 3
DILATIONS = (1, 4, 16)
STEPS = 128
HD = 64
ROT = HD // 4
ROPE_THETA = 500000.0
PH = 8
NK = 128
TOPK = 16
SLOTS_T = PH * TOPK
RMS_EPS = 1e-6
TAPS = 31
PE_TAPS = 12
BUCKETS = 32
MAX_DISTANCE = 128
NE = 16
NG = 4
EPG = NE // NG
FE = 512
LN_EPS = 1e-5
ALPHA = 4.0 ** 0.25
LAMBDA_INIT = 0.8 - 0.6 * math.exp(-0.3)
NEG = -1e30

CW = 2048
HW_ = CW // 2
RING = 6
ROUTING_STEPS = 10
WIDE_STEP = 1.6
MATCH_STEP = 2.2
_counts = [("c", 4), ("xc", 4), ("b", 4), ("q", 6), ("k", 6), ("v", 6), ("gc", 4), ("ga", 4),
           ("conv_out", 4), ("attn_out", 4), ("w_out", 4), ("wq", 8), ("down", 64), ("up", 64),
           ("pw1", 8), ("pw2", 4), ("moe0", 5 * 24), ("k2", 4), ("v2", 4), ("q2", 4),
           ("w_o", 4), ("moe1", 5 * 24)]
C0, _n = {}, 0
for _name, _k in _counts:
    C0[_name] = _n
    _n += _k
PASS = 48
TWO = 2 * C0["pw1"]

UNIT_BANKS = 3
_unit_counts = [(n, k) for n, k in _counts if n not in ("up", "moe0", "moe1")]
_unit_counts.insert([n for n, _ in _unit_counts].index("down"), ("keyscore", 8))
U0, _n = {}, 0
for _name, _k in _unit_counts:
    U0[_name] = _n
    _n += _k

_vecs = [("norm_mix", 8), ("conv_w", 24), ("gate_bias", 16), ("norm_ffn", 8), ("final_norm", 8),
         ("b_pw1", 16), ("w_dw", TAPS * 8), ("b_dw", 8), ("ln_g", 8), ("ln_b", 8), ("b_pw2", 8),
         ("ln_mix_g", 16), ("ln_mix_b", 16), ("ln_ffn_g", 16), ("ln_ffn_b", 16), ("subln_g", 1)]
V0, _n = {}, 0
for _name, _k in _vecs:
    V0[_name] = _n
    _n += _k
VECS = _n

_consts = [("ident", P), ("rot", P), ("iota", P), ("freq", 1), ("lower", EPG * EPG),
           ("before", P), ("ones", P), ("row", 1), ("base", 2 * NG), ("index", NG)]
K0, _n = {}, 0
for _name, _k in _consts:
    K0[_name] = _n
    _n += _k
CONSTS = _n
RELS = 384


def constants():
    pack = np.zeros((P, CONSTS), np.float32)
    pack[:, K0["ident"]:K0["ident"] + P] = np.eye(P)
    rot = np.zeros((P, P), np.float32)
    freq = np.zeros((P,), np.float32)
    half = ROT // 2
    inv = (ROPE_THETA ** (-np.arange(half) * (2.0 / ROT))).astype(np.float32)
    for m in range(P):
        d = m % HD
        if d < half:
            rot[m + half, m] = -1.0
        elif d < ROT:
            rot[m - half, m] = 1.0
        if d < ROT:
            freq[m] = inv[d % half]
    pack[:, K0["rot"]:K0["rot"] + P] = rot
    pack[:, K0["iota"]:K0["iota"] + P] = np.arange(P)[None]
    pack[:, K0["freq"]] = freq
    lower = np.tril(np.ones((EPG, EPG), np.float32), -1)
    pack[:, K0["lower"]:K0["lower"] + EPG * EPG] = lower.reshape(-1)[None]
    pack[:, K0["before"]:K0["before"] + P] = np.triu(np.ones((P, P)), 1)
    pack[:, K0["ones"]:K0["ones"] + P] = 1.0
    pack[:, K0["row"]] = np.arange(P)
    pack[:, K0["base"]:K0["base"] + 2 * NG] = np.tile(np.arange(NG) * P, 2)[None]
    pack[:, K0["index"]:K0["index"] + NG] = np.arange(NG)[None]
    rel = P + np.arange(P)[:, None] - np.arange(T)[None]
    mask = np.stack([np.where((rel >= 0) & (rel % r == 0) & (rel <= STEPS * r), 0.0, NEG)
                     for r in DILATIONS], 1)
    rels = (T - 1) - np.arange(RELS)
    exact = BUCKETS // 2
    nf = np.maximum(rels, 1).astype(np.float32)
    large = exact + (np.log(nf / exact) / math.log(MAX_DISTANCE / exact)
                     * (BUCKETS - exact)).astype(np.int32)
    bucket = np.where(rels < exact, np.maximum(rels, 0), np.minimum(large, BUCKETS - 1))
    onehot = np.zeros((BUCKETS + 1, RELS), np.float32)
    onehot[bucket, np.arange(RELS)] = 1.0
    onehot[BUCKETS] = np.where(rels >= 0, 0.0, NEG)
    slots = np.broadcast_to(np.arange(5 * P, dtype=np.float32), (P, 5 * P))
    return {"consts": pack, "mask": mask.astype(np.float32).reshape(P, -1), "onehot": onehot,
            "slots": np.ascontiguousarray(slots)}


def build(nc, t_x, t_w, t_vec, t_const, t_mask, t_onehot, t_slots, t_pos, t_keys, t_router,
          t_rbias, t_lam, t_rel, t_rows, t_out, dbg=None):
    ctx = ExitStack()
    with ctx:
        def sb(name, shape, dt=F32):
            return ctx.enter_context(nc.sbuf_tensor(name, shape, dt))

        def sem(name):
            return ctx.enter_context(nc.semaphore(name))

        with nc.sbuf_tensor("u", [P, DT, T], F32) as u:
            pass
        xh = sb("xh", [P, DT, T], F32R)
        xl = sb("xl", [P, DT, T], F32R)
        wh = sb("wh", [P, 2, HW_], F32R)
        wl = sb("wl", [P, 2, HW_], F32R)
        ring = sb("ring", [P, RING, HW_])
        h = sb("h", [P, DT, T])
        const = sb("const", [P, CONSTS])
        vec = sb("vec", [P, VECS])
        ones_d = sb("ones_d", [P, P])
        zeros = sb("zeros", [P, P], BF16)
        root = sb("root", [P, T])
        slot_t = sb("slot_t", [P, 3, T])
        router = sb("router", [P, DT, NE])
        rbias = sb("rbias", [P, NE])
        small = sb("small", [P, 384])
        eps = sb("eps", [P, 2])
        flags = sb("flags", [P, 2], I32)
        with nc.sbuf_tensor("big", [P, NK * T], F32) as big:
            pass
        wh2 = sb("wh2", [P, 4, HW_], F32R)
        wl2 = sb("wl2", [P, 4, HW_], F32R)
        pre_t = sb("pre_t", [P, DT * T + 2 * HALF + HALF])
        ATT, NRM = 10752, 10240
        with nc.sbuf_tensor("att_t", [P, ATT], F32) as att_t:
            pass
        gxh = sb("gxh", [P, DT, 5 * P], F32R)
        gxl = sb("gxl", [P, DT, 5 * P], F32R)
        spare = sb("spare", [P, ATT - 2 * DT * 5 * P])
        with nc.sbuf_tensor("norm_t", [P, NRM], F32) as norm_t:
            pass
        yh = sb("yh", [P, 5, D], F32R)
        yl = sb("yl", [P, 5, D], F32R)
        bank = [ctx.enter_context(nc.psum_tensor(f"bank{i}", [P, HALF], F32)) for i in range(8)]

        def C(name):
            return const[:, K0[name]:K0[name] + dict(_consts)[name]]

        def V(name, k):
            return vec[:, V0[name] + k:V0[name] + k + 1]

        ident = C("ident")

        class Region:

            def __init__(self, of, at, end):
                self.of, self.at, self.end = of, at, end

            def take(self, *shape):
                n = math.prod(shape)
                assert self.at + n <= self.end, (self.at, n, self.end)
                v = self.of[:, self.at:self.at + n]
                self.at += n
                names = "abcd"[:len(shape)]
                if len(shape) == 1:
                    return v
                return v.rearrange(f"p ({' '.join(names)}) -> p {' '.join(names)}",
                                   **{c: s for c, s in zip(names[1:], shape[1:])})

        r1 = Region(big, 0, NK * T)
        cgate = r1.take(DT, T)
        z = r1.take(DT, T + 2)
        conv = r1.take(DT, T)
        qk = r1.take(2 * GROUPS * 4, T)
        v1 = r1.take(TT, GROUPS * HEADS * HD)
        sig_c = r1.take(DT, T)
        sig_a = r1.take(DT, T)
        merged = r1.take(DT, T)
        o_t = r1.take(4, T)
        cos_t = r1.take(T)
        sin_t = r1.take(T)
        ang = r1.take(T)
        turn = r1.take(T)
        rot_tmp = r1.take(2, T)
        mask = r1.take(GROUPS, T)
        sc1 = r1.take(2, GROUPS, T)
        pr1 = r1.take(2, GROUPS, T)
        pt1 = r1.take(2, GROUPS * T)
        sq1 = cgate
        rows = qk.rearrange("p a b -> p (a b)")[:, 0:8 * RELS].rearrange("p (h r) -> p h r", h=8)
        act = big[:, :].rearrange("p (i t) -> p i t", t=T)
        rp = Region(big, 0, NK * T)
        pq = rp.take(PH * 2, T)
        keys = rp.take(PH * 2, P)
        TILES_BEFORE = 96
        rk = Region(big, TILES_BEFORE * T, NK * T)
        score = rk.take(TT, PH * 2, NK)
        rs = Region(big, TILES_BEFORE * T, NK * T)
        cand = rs.take(PH, TOPK * TOPK)
        match = rs.take(PH, TOPK, TOPK)
        top_v = rk.take(TT, PH * 2, TOPK)
        top_i = rk.take(TT, PH * 2, TOPK)
        top_f = rk.take(TT, PH * 2, TOPK)
        best = rk.take(TT, PH, TOPK)
        best_i = rk.take(TT, PH, TOPK)
        pos_a = rk.take(TT, SLOTS_T)
        pos_b = rk.take(TT, SLOTS_T)
        pos_f = rk.take(2, TT, SLOTS_T)
        slot = rk.take(3, TT, SLOTS_T)
        r2 = Region(pre_t, 0, DT * T + 2 * HALF + HALF)
        pre = r2.take(DT, T)
        silu = r2.take(HALF)
        hid = r2.take(HALF)
        rn = Region(norm_t, 0, NRM)
        cen = rn.take(DT, T)
        nrm = rn.take(DT, T)
        sq2 = rn.take(DT, T)
        glu = rn.take(DT, T + TAPS - 1)
        sg2 = rn.take(2, T)
        mtmp = cgate
        ra = Region(att_t, 0, ATT)
        k2 = ra.take(DT, T)
        v2 = ra.take(TT, D)
        q2 = ra.take(DT, T)
        relb = ra.take(HEADS, T)
        sc2 = ra.take(2, 2, T)
        pr2 = ra.take(2, 2, T)
        pt2 = ra.take(2, T)
        at_out = k2
        diag = k2.rearrange("p a (b c) -> p (a b) c", c=P)
        DIAGS = DT * T // P
        xth = xh[:, :, :].rearrange("p a b -> p (a b)").rearrange("p (t d) -> p t d", t=TT)
        xtl = xl[:, :, :].rearrange("p a b -> p (a b)").rearrange("p (t d) -> p t d", t=TT)
        whf = wh[:, :, :].rearrange("p a b -> p (a b)")
        wlf = wl[:, :, :].rearrange("p a b -> p (a b)")
        pick_t = whf[:, 0:TT * 5 * P].rearrange("p (t s) -> p t s", t=TT)
        pick_s = wlf[:, 0:5 * T].rearrange("p (i t) -> p i t", i=5)
        hid_h = whf[:, TT * 5 * P:TT * 5 * P + FE].rearrange("p (f s) -> p f s", f=4)
        hid_l = wlf[:, 5 * T:5 * T + FE].rearrange("p (f s) -> p f s", f=4)
        slot_no = slot_t[:, :, :].rearrange("p a b -> p (a b)")[:, 0:5 * P]
        neg_max = small[:, 0:4]
        denom = small[:, 4:8]
        rden = small[:, 8:12]
        lam = small[:, 12:16]
        sumsq = small[:, 16:32]
        sub_g = small[:, 32:33]
        mx8 = small[:, 33:34]
        aff = small[:, 64:96].rearrange("p (a b) -> p a b", a=TT)
        sel = small[:, 96:128].rearrange("p (a b) -> p a b", a=TT)
        top2 = small[:, 128:160].rearrange("p (a b) -> p a b", a=TT)
        rank = small[:, 160:192]
        gscore = small[:, 192:200]
        grank = small[:, 200:208]
        gates = small[:, 208:240].rearrange("p (a b) -> p a b", a=TT)
        wsum = small[:, 240:242]
        gsum = small[:, 256:272].rearrange("p (a b) -> p a b", a=TT)
        gsel = small[:, 272:304].rearrange("p (a b) -> p a b", a=TT)
        place = small[:, 304:306]
        first = small[:, 306:308]
        fits = small[:, 308:310]
        slot_id = small[:, 310:312]
        tmp8 = small[:, 312:320]
        tmp8b = small[:, 320:328]
        over = small[:, 328:332]
        over_i = small[:, 332:336]
        flag_f = small[:, 336:338]
        slot_gate = sb("slot_gate", [P, 5 * NE])
        rden2 = sb("rden2", [P, HEADS * TT, 2])
        lamp = cen

        w_ready = [sem(f"w_ready{i}") for i in range(RING)]
        hi_ready = sem("hi_ready")
        lo_ready = sem("lo_ready")
        half_done = sem("half_done")
        xh_ready = sem("xh_ready")
        x_ready = sem("x_ready")
        diag_made = sem("diag_made")
        diag_used = sem("diag_used")
        ah_ready = sem("ah_ready")
        a_ready = sem("a_ready")
        hid32 = sem("hid32")
        hid_hi = sem("hid_hi")
        unit_free = [sem(f"unit_free{i}") for i in range(UNIT_BANKS)]
        loaded = sem("loaded")
        x_loaded = sem("x_loaded")
        keys_loaded = sem("keys_loaded")
        two_loaded = sem("two_loaded")
        rel_loaded = sem("rel_loaded")
        set_up = sem("set_up")
        rows_ready = sem("rows_ready")
        rows_copied = sem("rows_copied")
        rows_stored = sem("rows_stored")
        stat_in = sem("stat_in")
        stat_out = sem("stat_out")
        centred = sem("centred")
        squared = sem("squared")
        root_ready = sem("root_ready")
        scaled = sem("scaled")
        norm_done = sem("norm_done")
        angles_ready = sem("angles_ready")
        rope_ready = sem("rope_ready")
        rot_ready = sem("rot_ready")
        rot_done = sem("rot_done")
        s_ready = sem("s_ready")
        s_read = sem("s_read")
        max_ready = sem("max_ready")
        exp_done = sem("exp_done")
        p_ready = sem("p_ready")
        t_ready = sem("t_ready")
        pt_ready = sem("pt_ready")
        pv_done = sem("pv_done")
        o_done = sem("o_done")
        key_s = sem("key_s")
        best_ready = sem("best_ready")
        best_exp = sem("best_exp")
        slots_ready = sem("slots_ready")
        slots_t = sem("slots_t")
        slots_copied = sem("slots_copied")
        keys_matched = [[sem(f"keys_matched{c}{i}") for i in range(2)] for c in range(2)]
        scattered = [sem(f"scattered{i}") for i in range(2)]
        weighted = [sem(f"weighted{i}") for i in range(2)]
        gated = [sem(f"gated{i}") for i in range(2)]
        acc_zero = sem("acc_zero")
        act_read = sem("act_read")
        res_done = sem("res_done")
        glu_sig = sem("glu_sig")
        mix_b = sem("mix_b")
        logits = sem("logits")
        affin = sem("affin")
        gates_ready = sem("gates_ready")
        groups_ready = sem("groups_ready")
        places_ready = sem("places_ready")
        flags_ready = sem("flags_ready")
        slots_made = sem("slots_made")
        slot_row = sem("slot_row")
        picks_ready = sem("picks_ready")
        xt_t = sem("xt_t")
        xt_hi = sem("xt_hi")
        xt_lo = sem("xt_lo")
        gat_ready = sem("gat_ready")
        gat_hi = sem("gat_hi")
        gat_lo = sem("gat_lo")
        sg_ready = sem("sg_ready")
        xg_hi = sem("xg_hi")
        xg_ready = sem("xg_ready")
        silu_done = sem("silu_done")
        t_done = sem("t_done")
        hid_done = sem("hid_done")
        y_hi = sem("y_hi")
        y_done = sem("y_done")
        y_cleared = sem("y_cleared")
        back = sem("back")
        lam_exp = sem("lam_exp")
        lam_sum = sem("lam_sum")
        sub_sum = sem("sub_sum")
        sub_root = sem("sub_root")
        sub_scaled = sem("sub_scaled")
        sub_t = sem("sub_t")
        sub_out = sem("sub_out")
        out_stored = sem("out_stored")
        dve_step = sem("dve_step")
        act_step = sem("act_step")

        NORMS = {n: i + 1 for i, n in enumerate(
            ["mix", "ffn", "final", "conv", "mix0", "ffn0", "mix1", "ffn1"])}
        STATS = {"mix": 1, "ffn": 2, "final": 3, "conv": 4, "mix0": 6, "ffn0": 8, "mix1": 10, "ffn1": 12}
        ROOTS = NORMS
        LNS = {"conv": 1, "mix0": 2, "ffn0": 3, "mix1": 4, "ffn1": 5}
        SPLITS = {n: i for i, n in enumerate(["mix", "conv", "attn", "merged", "ffn", "final", "silu",
                                              "kvq", "at_out"])}
        RES = {"mixer": 1, "experts": 2, "pw2": 3, "moe0": 4, "w_o": 5, "moe1": 6}

        def unit_bank(unit):
            return bank[unit % UNIT_BANKS]

        def rows_bank(unit, tt):
            return bank[unit % UNIT_BANKS + (5 if tt else 0)]

        def evacuated(eng, unit):
            eng.wait_ge(unit_free[unit % UNIT_BANKS], unit // UNIT_BANKS + 1)

        def computed(eng, name, j):
            eng.wait_ge(half_done, 2 * (C0[name] + j + 1))

        def parts(x):
            if x < TWO:
                return wh[:, x % 2, :], wl[:, x % 2, :], 2
            return wh2[:, x % 4, :], wl2[:, x % 4, :], 4

        def split_hi(sc, x, turns=0, per=6):
            hi, _, n = parts(x)
            sc.wait_ge(w_ready[x % RING], (turns * (per // RING) + x // RING + 1) * 16)
            if x >= n:
                sc.wait_ge(half_done, turns * per + x - n + 1)
            nc.scalar.activation(hi, ring[:, x % RING, :], ACT.Copy).then_inc(hi_ready, 1)

        def split_lo(ve, x, turns=0, per=6):
            hi, lo, _ = parts(x)
            ve.wait_ge(hi_ready, turns * per + x + 1)
            nc.vector.tensor_tensor(lo, ring[:, x % RING, :], hi.bitcast(F32), ALU.subtract)\
                .then_inc(lo_ready, 1)

        def halves_ahead(name, j):
            c = C0[name] + j
            if 2 * c < TWO:
                return [x for x in (2 * c + 2, 2 * c + 3) if x < TWO]
            end = 2 * C0["moe0" if c < C0["moe0"] else "moe1"]
            return [x for x in (2 * c + 4, 2 * c + 5) if x < end]

        def split_x_hi(sc, name, src, kt=DT):
            q = kt // 4
            for i in range(4):
                nc.scalar.activation(xh[:, i * q:(i + 1) * q, :], src[:, i * q:(i + 1) * q, :],
                                     ACT.Copy).then_inc(xh_ready, 1)

        def split_x_lo(ve, name, src, kt=DT):
            q = kt // 4
            for i in range(4):
                ve.wait_ge(xh_ready, 4 * SPLITS[name] + i + 1)
                nc.vector.tensor_tensor(xl[:, i * q:(i + 1) * q, :], src[:, i * q:(i + 1) * q, :],
                                        xh[:, i * q:(i + 1) * q, :].bitcast(F32), ALU.subtract)\
                    .then_inc(x_ready, 1)

        def o_rows(qt):
            return (cen if qt == 0 else nrm).rearrange("p a b -> p (a b)")[:, 0:D]

        def onehots(half):
            rows_ = u[:, half * 4:half * 4 + 4, :].rearrange("p a (r k) -> p (a r) k", k=P)
            return rows_[:, 0:4, :], rows_[:, 4:8, :]

        block = ctx.enter_context(nc.Block())

        @block.sync
        def _(sp):
            def load(half, place):
                slot = place % RING if isinstance(place, int) else None
                assert slot is not None
                load_at(half, slot)

            def load_at(half, slot):
                sp.dma_start(ring[:, slot, :].unsqueeze(1),
                             t_w[bass.ds(half, 1)].rearrange("c p n -> p c n"))\
                    .then_inc(w_ready[slot], 16)

            def run(x, count, half):
                turns_ = count // RING
                if turns_ > 0:
                    with sp.Fori(0, turns_) as t:
                        for j in range(RING):
                            sp.wait_ge(lo_ready, t * RING + x + j - RING + 1)
                            load_at(t * RING + half + j, (x + j) % RING)
                for j in range(turns_ * RING, count):
                    sp.wait_ge(lo_ready, x + j - RING + 1)
                    load_at(half + j, (x + j) % RING)

            for slot in range(RING):
                load_at(slot, slot)
            x, half = RING, RING
            for layer in range(2):
                start = 2 * C0[f"moe{layer}"]
                run(x, start + 4 - x, half)
                half += start + 8 - x
                first_half = half - 8
                run(start + 4, 4 * PASS - 8, half)
                half += 4 * PASS - 4
                run(start + 4 * PASS - 4, 4, half)
                half += 4
                x = start + 4 * PASS
                sp.wait_ge(flags_ready, layer + 1)
                fifth = sp.value_load(flags[0:1, 0:1], min_val=0, max_val=1)
                group = sp.value_load(flags[0:1, 1:2], min_val=0, max_val=NG - 1)
                with sp.If(fifth > 0):
                    run(x, 4, group * PASS + first_half)
                    run(x + 4, PASS - 8, group * PASS + (first_half + 8))
                    run(x + PASS - 4, 4, group * PASS + (first_half + PASS + 4))
                with sp.Else():
                    for j in range(RING):
                        slot = (x + j) % RING
                        sp.wait_ge(w_ready[slot], (x + j) // RING * 16)
                        sp.sem_inc(w_ready[slot], PASS // RING * 16)
                x += PASS
            sp.wait_ge(norm_done, NORMS["ffn1"])
            sp.dma_start(t_out, h[:, :, :]).then_inc(out_stored, 16)
            sp.wait_ge(out_stored, 16)

        @block.gpsimd
        def _(pool):
            pool.dma_start(h[:, :, :], t_x).then_inc(x_loaded, 16)
            pool.dma_start(const[:, :], t_const).then_inc(loaded, 16)
            pool.dma_start(vec[:, :], t_vec).then_inc(loaded, 16)
            pool.dma_start(ang.bitcast(I32), t_pos.partition_broadcast(P)).then_inc(loaded, 16)
            pool.dma_start(mask, t_mask.rearrange("p (g k) -> p g k", g=GROUPS)).then_inc(loaded, 16)
            pool.dma_start(u[0:BUCKETS + 1, 0, :], t_onehot[:, 0:T]).then_inc(loaded, 16)
            pool.dma_start(u[0:BUCKETS + 1, 1, 0:RELS - T], t_onehot[:, T:RELS]).then_inc(loaded, 16)
            nc.gpsimd.memset(u[0:BUCKETS + 1, 2, 0:HEADS], 1.0).then_inc(set_up, 1)
            pool.wait_ge(set_up, 1)
            pool.dma_start(u[0:BUCKETS, 2, 0:HEADS], t_rel).then_inc(loaded, 16)
            pool.dma_start(router[:, :, :], t_router).then_inc(loaded, 16)
            pool.dma_start(rbias[:, :], t_rbias.partition_broadcast(P)).then_inc(loaded, 16)
            nc.gpsimd.memset(ones_d[:, :], 1.0 / D).then_inc(set_up, 1)
            nc.gpsimd.memset(zeros[:, :], 0.0).then_inc(set_up, 1)
            nc.gpsimd.memset(eps[:, 0:1], RMS_EPS).then_inc(set_up, 1)
            nc.gpsimd.memset(eps[:, 1:2], LN_EPS).then_inc(set_up, 1)
            nc.gpsimd.memset(z[:, :, 0:2], 0.0).then_inc(set_up, 1)
            pool.wait_ge(rows_copied, HEADS)
            pool.dma_start(t_rows.rearrange("h p r -> p h r"), rows).then_inc(rows_stored, 16)
            pool.wait_ge(norm_done, NORMS["ffn"])
            pool.dma_start(keys, t_keys).then_inc(keys_loaded, 16)
            pool.wait_ge(norm_done, NORMS["final"])
            pool.wait_ge(rows_stored, 16)
            pool.dma_start(lamp[:, 0, :], t_lam.partition_broadcast(P)).then_inc(two_loaded, 16)
            pool.dma_start(slot_no, t_slots).then_inc(two_loaded, 16)
            for layer in range(2):
                pool.wait_ge(norm_done, NORMS[f"mix{layer}"])
                nc.gpsimd.memset(yh[:, 4, :].bitcast(F32), 0.0).then_inc(y_cleared, 1)
                nc.gpsimd.memset(yl[:, 4, :].bitcast(F32), 0.0).then_inc(y_cleared, 1)
                if layer == 0:
                    pool.wait_ge(norm_done, NORMS["ffn0"])
                    for hd in range(HEADS):
                        row = t_rows[hd].rearrange("p r -> (p r)")
                        skew = row[P - 1:P - 1 + P * (RELS - 1)].rearrange("(p r) -> p r", r=RELS - 1)
                        pool.dma_start(relb[:, hd, :], skew[:, 0:T]).then_inc(rel_loaded, 16)

        @block.tensor
        def _(pe):
            def free_unit(unit, turns=0):
                if unit >= UNIT_BANKS:
                    pe.wait_ge(unit_free[unit % UNIT_BANKS], turns + unit // UNIT_BANKS)

            def arrived(x, turns=0, per=6):
                pe.wait_ge(lo_ready, turns * per + x + 1)
                return parts(x)[0:2]

            def split_in(name, k, kt):
                if name is not None and k % (kt // 4) == 0:
                    pe.wait_ge(x_ready, 4 * SPLITS[name] + k // (kt // 4) + 1)

            def three(out, w, x, start, stop, **kw):
                nc.tensor.matmul(out, w[0], x[0], start=start, stop=False, **kw)
                nc.tensor.matmul(out, w[0], x[1], start=False, stop=False, **kw)
                return nc.tensor.matmul(out, w[1], x[0], start=False, stop=stop, **kw)

            def project(name, j, split=None, kt=DT, turns=0):
                chunk, unit = C0[name] + j, U0[name] + j
                free_unit(unit, turns)
                for n in range(2):
                    w = [v[:, 0:kt * P].rearrange("p (k n) -> p k n", k=kt)
                         for v in arrived(2 * chunk + n, turns)]
                    for k in range(kt):
                        if j == 0 and n == 0:
                            split_in(split, k, kt)
                        last = three(unit_bank(unit)[:, n * T:(n + 1) * T],
                                     [v[:, k, :] for v in w], [v[:, k, :] for v in (xh, xl)],
                                     k == 0, k == kt - 1)
                    last.then_inc(half_done, 1)

            def project_rows(name, j):
                chunk, unit = C0[name] + j, U0[name] + j
                free_unit(unit)
                for n in range(2):
                    w = [v.rearrange("p (k n) -> p k n", k=4) for v in arrived(2 * chunk + n)]
                    for tt in range(TT):
                        for k in range(4):
                            last = three(rows_bank(unit, tt)[:, 0:T],
                                         [v[:, 4 * n + k, tt * P:(tt + 1) * P] for v in (xh, xl)],
                                         [v[:, k, :] for v in w], n + k == 0, n + k == 4)
                    last.then_inc(half_done, 1)

            def mean(n, src, arrived_=None):
                pe.wait_ge(stat_in, arrived_ or n)
                for k in range(DT):
                    last = nc.tensor.matmul(bank[3][:, 0:T], ones_d[:, :], src[:, k, :],
                                            start=(k == 0), stop=(k == DT - 1))
                last.then_inc(stat_out, 1)

            def ln_means(name):
                n = LNS[name]
                mean(STATS[name], pre, STATS[name] - (n - 1))
                for k in range(DT):
                    if k % 2 == 0:
                        pe.wait_ge(squared, 4 * (n - 1) + k // 2 + 1)
                    last = nc.tensor.matmul(bank[7][:, 0:T], ones_d[:, :], sq2[:, k, :],
                                            start=(k == 0), stop=(k == DT - 1))
                last.then_inc(stat_out, 1)

            pe.wait_ge(set_up, 6)
            mean(STATS["mix"], sq1)
            pe.wait_ge(loaded, 9 * 16)
            for hd in range(HEADS):
                lhs = u[0:BUCKETS + 1, 2, hd:hd + 1].broadcast_to([BUCKETS + 1, P])
                if hd == 3:
                    pe.wait_ge(root_ready, ROOTS["mix"])
                nc.tensor.matmul(bank[hd][:, 0:T], lhs, u[0:BUCKETS + 1, 0, :], start=True, stop=True)
                nc.tensor.matmul(bank[hd][:, T:RELS], lhs, u[0:BUCKETS + 1, 1, 0:RELS - T],
                                 start=True, stop=True).then_inc(rows_ready, 1)
            pe.wait_ge(rows_copied, HEADS)
            for name in ("c", "xc", "b"):
                for j in range(4):
                    project(name, j, "mix" if name == "c" else None)

            def rotate(j):
                evacuated(pe, U0["q"] + j)
                if j >= 2:
                    pe.wait_ge(rot_done, j - 1)
                nc.tensor.matmul(bank[3 + j % 2][:, :], C("rot"), qk[:, 2 * j:2 * j + 2, :],
                                 start=True, stop=True).then_inc(rot_ready, 1)

            for j in range(12):
                project("q", j) if j < 6 else project("k", j - 6)
                if j >= 1:
                    rotate(j - 1)
            project_rows("v", 0)
            rotate(11)
            for j in range(1, 6):
                project_rows("v", j)
            for name in ("gc", "ga"):
                for j in range(4):
                    project(name, j)
            for j in range(4):
                project("conv_out", j, "conv")

            pe.wait_ge(rot_done, 12)
            for b_ in range(6):
                evacuated(pe, U0["v"] + b_)
            tiles = [(hd, qt) for hd in range(HEADS) for qt in range(TT)]

            def scores(i):
                hd, qt = tiles[i]
                row, n = hd % 2 * HD, (qt + 1) * P
                if i >= 2:
                    pe.wait_ge(s_read, i - 1)
                for g in range(GROUPS):
                    ft = g * 4 + hd // 2
                    out = bank[3 + i % 2 * 2 + g // 2][:, g % 2 * T:g % 2 * T + n]
                    last = nc.tensor.matmul(out, qk[row:row + HD, ft, qt * P:(qt + 1) * P],
                                            qk[row:row + HD, 12 + ft, 0:n], start=True, stop=True)
                last.then_inc(s_ready, 1)

            tb = [(0, 1), (2, 7)]

            def blocks(i):
                return [(g, kt) for g in range(GROUPS) for kt in range(tiles[i][1] + 1)]

            def transposes(i):
                pe.wait_ge(p_ready, i + 1)
                if i >= 2:
                    pe.wait_ge(o_done, i - 1)
                for n, (g, kt) in enumerate(blocks(i)):
                    last = nc.tensor.transpose(bank[tb[i % 2][n // 4]][:, n % 4 * P:n % 4 * P + P],
                                               pr1[:, i % 2, g, kt * P:(kt + 1) * P], ident)
                last.then_inc(t_ready, 1)

            def values(i):
                hd, qt = tiles[i]
                pe.wait_ge(pt_ready, i + 1)
                bl = blocks(i)
                for n, (g, kt) in enumerate(bl):
                    at = (g * HEADS + hd // 2 * 2) * HD
                    last = nc.tensor.matmul(bank[tb[i % 2][1]][:, T:T + P], v1[:, kt, at:at + P],
                                            pt1[:, i % 2, n * P:(n + 1) * P],
                                            start=(n == 0), stop=(n == len(bl) - 1))
                last.then_inc(pv_done, 1)

            for unit in range(U0["attn_out"] - UNIT_BANKS, U0["attn_out"]):
                evacuated(pe, unit)
            scores(0)
            scores(1)
            for i in range(len(tiles)):
                if i + 2 < len(tiles):
                    scores(i + 2)
                if i >= 1:
                    values(i - 1)
                transposes(i)
            values(len(tiles) - 1)

            pe.wait_ge(o_done, len(tiles))
            for j in range(4):
                project("attn_out", j, "attn", kt=4)
            for j in range(4):
                project("w_out", j, "merged")
            mean(STATS["ffn"], sq1)
            for j in range(8):
                project("wq", j, "ffn")
            pe.wait_ge(keys_loaded, 16)
            for b_ in range(3):
                evacuated(pe, U0["wq"] + 5 + b_)
            for j in range(8):
                tt, part = j // 4, j % 4
                free_unit(U0["keyscore"] + j)
                for c in range(4):
                    last = nc.tensor.matmul(unit_bank(U0["keyscore"] + j)[:, c * NK:(c + 1) * NK],
                                            pq[:, part * 4 + c, tt * P:(tt + 1) * P],
                                            keys[:, part * 4 + c, :], start=True, stop=True)
                last.then_inc(key_s, 1)
            with pe.Fori(0, TILES_BEFORE // 6) as it:
                for j in range(3):
                    project("down", j, turns=it)
            pe.wait_ge(slots_ready, 1)
            for n in range(3):
                for tt in range(TT):
                    last = nc.tensor.transpose(bank[4 + n][:, tt * P:(tt + 1) * P],
                                               slot[:, n, tt, :], ident)
                last.then_inc([scattered[0], scattered[1], slots_t][n], 1)
            with pe.Fori(TILES_BEFORE // 6, 21) as it:
                for j in range(3):
                    project("down", j, turns=it)
            project("down", 63)
            pe.wait_ge(slots_copied, 1)
            with pe.Fori(0, T // 8) as it:
                for half in range(2):
                    a, b = onehots(half)
                    pe.wait_ge(gated[half], it + 1)
                    pe.wait_ge(keys_matched[0][half], it + 1)
                    out = bank[4 + half][:, :].rearrange("p (i t) -> p t i", t=4)
                    for tk in range(4):
                        pe.wait_ge(weighted[half], it * 4 + (tk + 1))
                        last = nc.tensor.matmul(out[:, tk, :], b[:, tk, :], a[:, tk, :],
                                                start=True, stop=True)
                    last.then_inc(scattered[half], 1)
            for half in range(2):
                pe.wait_ge(gated[half], T // 8 + 1)

            def zero_acc():
                for b_ in range(4, 8):
                    nc.tensor.matmul(bank[b_][:, :], zeros[:, :],
                                     zeros[:, :].unsqueeze(1).broadcast_to([P, 4, P]),
                                     start=True, stop=False, skip_group_check=True)

            def accumulate(x, src, turns=0, final=False):
                w = arrived(x, turns)
                for n in range(DT):
                    last = three(bank[4 + n // 2][:, n % 2 * T:n % 2 * T + T],
                                 [v[:, n * P:(n + 1) * P] for v in w], src,
                                 False, final and n % 2 == 1, skip_group_check=True)
                last.then_inc(half_done, 1)

            def up(j, turns=0):
                pe.wait_ge(a_ready, turns * 3 + j + 1)
                for k in range(2):
                    at = (2 * j + k) % 6
                    accumulate(2 * (C0["up"] + j) + k, [xh[:, at, :], xl[:, at, :]], turns,
                               final=(j == 63 and k == 1))

            zero_acc()
            with pe.Fori(0, 21) as it:
                for j in range(3):
                    up(j, it)
            up(63)
            mean(STATS["final"], sq2)

            for j in range(8):
                project("pw1", j, "final")
                for pair_ in ([j // 2 - 1] if j in (2, 4, 6) else [3] if j == 7 else []):
                    for k in (2 * pair_, 2 * pair_ + 1):
                        evacuated(pe, U0["pw1"] + k)
                        for i in range(PE_TAPS):
                            n = k * PE_TAPS + i
                            pe.wait_ge(diag_made, n + 1)
                            nc.tensor.matmul(bank[4 + pair_][:, k % 2 * T:k % 2 * T + T],
                                             diag[:, n % DIAGS, :], glu[:, k, i:i + T],
                                             start=(i == 0), stop=(i == PE_TAPS - 1))\
                                .then_inc(diag_used, 1)
            ln_means("conv")
            for j in range(4):
                project("pw2", j, "silu")

            def layer_norm(name):
                ln_means(name)
                pe.wait_ge(norm_done, NORMS[name])

            def one_pass(layer, p, more):
                x0, q = 2 * C0[f"moe{layer}"] + 4, p + 5 * layer
                n0 = q * 4 + 1

                def down_(e, at):
                    pe.wait_ge(hid_done, n0 + e + 1)
                    if e == 0:
                        pe.wait_ge(y_done, q + 1)
                    for i in range(4):
                        w = arrived(x0 + at + i, p, PASS)
                        for c in range(2):
                            last = three(bank[4 + c][:, :], [v[:, i, :] for v in (hid_h, hid_l)],
                                         [v[:, c * HALF:(c + 1) * HALF] for v in w],
                                         e + i == 0, e == 3 and i == 3)
                        last.then_inc(half_done, 1)

                def flip(e):
                    pe.wait_ge(hid32, n0 + e + 1)
                    pe.wait_ge(hid_done, n0 + e)
                    for f in range(4):
                        last = nc.tensor.transpose(bank[2][:, f * P:(f + 1) * P],
                                                   hid[:, f * P:(f + 1) * P], ident)
                    last.then_inc(t_done, 1)

                up_(layer, p, 0, 1, 0)
                for e in range(1, 4):
                    up_(layer, p, e, 0, 12 * e - 8)
                    if e == 1:
                        flip(0)
                    up_(layer, p, e, 1, 12 * e - 4)
                    down_(e - 1, 12 * e)
                    flip(e)
                if more:
                    pe.wait_ge(xg_ready, q + 2)
                    up_(layer, p, 4, 0, 40)
                down_(3, 44 if more else 40)

            def up_(layer, p, e, which, at):
                x0, n = 2 * C0[f"moe{layer}"] + 4, (p + 5 * layer) * 4 + 1 + e
                if which == 0:
                    pe.wait_ge(silu_done, n)
                else:
                    pe.wait_ge(hid32, n)
                for i in range(4):
                    w = [v.rearrange("p (k n) -> p k n", k=2)
                         for v in arrived(x0 + at + i, p, PASS)]
                    for k in range(2):
                        last = three(bank[which][:, :], [v[:, 2 * i + k, 0:P] for v in (xh, xl)],
                                     [v[:, k, :] for v in w], i + k == 0, i + k == 4)
                    last.then_inc(half_done, 1)

            def experts(layer):
                for tt in range(TT):
                    for k in range(DT):
                        last = nc.tensor.matmul(bank[3][:, tt * NE:(tt + 1) * NE],
                                                h[:, k, tt * P:(tt + 1) * P], router[:, k, :],
                                                start=(k == 0), stop=(k == DT - 1))
                last.then_inc(logits, 1)
                for tt in range(TT):
                    for half in range(2):
                        for k in range(4):
                            last = nc.tensor.transpose(bank[4 + 2 * tt + half][:, k * P:(k + 1) * P],
                                                       h[:, 4 * half + k, tt * P:(tt + 1) * P], ident)
                        last.then_inc(xt_t, 1)
                pe.wait_ge(groups_ready, layer + 1)
                g0, g1 = grank[:, 0:NG], grank[:, NG:2 * NG]
                for at, terms in ((32, [("before", g0)]), (36, [("ones", g0), ("before", g1)]),
                                  (40, [("ones", g0), ("ones", g1)])):
                    for i, (m, g) in enumerate(terms):
                        last = nc.tensor.matmul(bank[3][:, at:at + NG], C(m), g,
                                                start=(i == 0), stop=(i == len(terms) - 1))
                last.then_inc(places_ready, 1)
                pe.wait_ge(slots_made, layer + 1)
                for tt in range(TT):
                    last = nc.tensor.matmul(bank[3][:, T + tt * P:T + (tt + 1) * P], C("ones"),
                                            silu[:, tt * P:(tt + 1) * P], start=True, stop=True)
                last.then_inc(slot_row, 1)
                for i in range(5):
                    for tt in range(TT):
                        last = nc.tensor.matmul(bank[2][:, i * NE:(i + 1) * NE],
                                                pick_t[:, tt, i * P:(i + 1) * P].bitcast(F32),
                                                gates[:, tt, :], start=(tt == 0), stop=(tt == 1))
                last.then_inc(sg_ready, 1)
                pe.wait_ge(xt_hi, 4 * layer + 4)
                pe.wait_ge(xt_lo, 4 * layer + 4)
                for k in range(DT):
                    b_ = [(4, 5, 6), (7, 0, 1)][k % 2]
                    if k >= 2:
                        pe.wait_ge(gat_hi, DT * layer + k - 1)
                        pe.wait_ge(gat_lo, DT * layer + k - 1)
                    for c, v in enumerate((xth, xtl)):
                        for out, s0, s1 in ((bank[b_[c]][:, :], 0, 4 * P),
                                            (bank[b_[2]][:, c * P:(c + 1) * P], 4 * P, 5 * P)):
                            for tt in range(TT):
                                last = nc.tensor.matmul(out, v[:, tt, k * P:(k + 1) * P],
                                                        pick_t[:, tt, s0:s1],
                                                        start=(tt == 0), stop=(tt == 1))
                    last.then_inc(gat_ready, 1)
                pe.wait_ge(gat_hi, DT * (layer + 1))
                pe.wait_ge(gat_lo, DT * (layer + 1))
                pe.wait_ge(xg_ready, 5 * layer + 1)
                up_(layer, 0, 0, 0, -4)
                with pe.Fori(0, 3) as p:
                    one_pass(layer, p, True)
                one_pass(layer, 3, False)
                fifth = pe.value_load(flags[0:1, 0:1], min_val=0, max_val=1)
                with pe.If(fifth > 0):
                    pe.wait_ge(xg_ready, 5 * layer + 5)
                    up_(layer, 4, 0, 0, -4)
                    one_pass(layer, 4, False)
                with pe.Else():
                    pe.wait_ge(half_done, 2 * C0[f"moe{layer}"] + 4 * PASS)
                    pe.sem_inc(half_done, PASS)
                    pe.sem_inc(t_done, 4)
                pe.wait_ge(y_done, 5 * (layer + 1) + 1)
                pe.wait_ge(y_cleared, 2 * (layer + 1))
                pe.wait_ge(picks_ready, layer + 1)
                for n in range(DT):
                    out = bank[[6, 7, 0, 1][n // 2]][:, n % 2 * T:n % 2 * T + T]
                    for i in range(5):
                        for c, v in enumerate((yh, yl)):
                            last = nc.tensor.matmul(out, v[:, i, n * P:(n + 1) * P], pick_s[:, i, :],
                                                    start=(i + c == 0), stop=(i + c == 5))
                    if n % 2 == 1:
                        last.then_inc(back, 1)

            layer_norm("mix0")
            experts(0)
            layer_norm("ffn0")
            for j in range(4):
                project("k2", j, "kvq")
            for j in range(4):
                project_rows("v2", j)
            for j in range(4):
                project("q2", j)
            for unit in range(U0["w_o"] - 3, U0["w_o"]):
                evacuated(pe, unit)
            n1 = len(tiles)

            def scores2(i):
                hd, qt = tiles[i]
                if i >= 2:
                    pe.wait_ge(s_read, n1 + i - 1)
                row, n = hd % 2 * HD, (qt + 1) * P
                for c in range(2):
                    ft = c * 4 + hd // 2
                    last = nc.tensor.matmul(bank[3 + i % 2][:, c * T:c * T + n],
                                            q2[row:row + HD, ft, qt * P:(qt + 1) * P],
                                            k2[row:row + HD, ft, 0:n], start=True, stop=True)
                last.then_inc(s_ready, 1)

            def transposes2(i):
                pe.wait_ge(p_ready, n1 + i + 1)
                if i >= 2:
                    pe.wait_ge(o_done, n1 + i - 1)
                for kt in range(tiles[i][1] + 1):
                    last = nc.tensor.transpose(bank[5 + i % 2][:, kt * P:(kt + 1) * P],
                                               pr2[:, i % 2, 0, kt * P:(kt + 1) * P], ident)
                last.then_inc(t_ready, 1)

            def values2(i):
                hd, qt = tiles[i]
                pe.wait_ge(pt_ready, n1 + i + 1)
                for kt in range(qt + 1):
                    last = nc.tensor.matmul(bank[5 + i % 2][:, T:T + P],
                                            pt2[:, i % 2, kt * P:(kt + 1) * P],
                                            v2[:, kt, hd * P:(hd + 1) * P],
                                            start=(kt == 0), stop=(kt == qt))
                last.then_inc(pv_done, 1)

            scores2(0)
            scores2(1)
            for i in range(n1):
                if i + 2 < n1:
                    scores2(i + 2)
                if i >= 1:
                    values2(i - 1)
                transposes2(i)
            values2(n1 - 1)
            pe.wait_ge(sub_scaled, 1)
            for hd in range(HEADS):
                for qt in range(TT):
                    last = nc.tensor.transpose(bank[hd // 2][:, hd % 2 * T + qt * P:hd % 2 * T + qt * P + P],
                                               o_rows(qt)[:, hd * P:(hd + 1) * P], ident)
                if hd % 2 == 1:
                    last.then_inc(sub_t, 1)
            pe.wait_ge(sub_out, 4)
            for j in range(4):
                project("w_o", j, "at_out")
            layer_norm("mix1")
            experts(1)
            layer_norm("ffn1")

        @block.scalar
        def _(sc):
            step = [0]

            def own(ins):
                step[0] += 1
                ins.then_inc(act_step, 1)
                sc.wait_ge(act_step, step[0])

            act_ = nc.scalar.activation

            def square(src, dst):
                act_(dst, src, ACT.Square).then_inc(stat_in, 1)

            def sqrt_mean(stat, e):
                sc.wait_ge(stat_out, stat)
                act_(root[:, :], bank[7 if e else 3][:, 0:T], ACT.Sqrt, bias=eps[:, e:e + 1])\
                    .then_inc(root_ready, 1)

            def free(ins, unit):
                ins.then_inc(unit_free[unit % UNIT_BANKS], 1)

            def ahead(name, j, turns=0):
                for x in halves_ahead(name, j):
                    split_hi(sc, x, turns)

            sc.sem_inc(silu_done, 1)
            sc.sem_inc(y_hi, 1)
            sc.wait_ge(x_loaded, 16)
            square(h[:, :, :], sq1)
            split_hi(sc, 0)
            split_hi(sc, 1)
            sc.wait_ge(set_up, 6)
            sqrt_mean(STATS["mix"], 0)
            sc.wait_ge(angles_ready, 1)
            act_(sin_t, ang, ACT.Sin).then_inc(rope_ready, 1)
            act_(cos_t, ang, ACT.Sin, scale=0.5).then_inc(rope_ready, 1)
            for hd in range(HEADS):
                sc.wait_ge(rows_ready, hd + 1)
                act_(rows[:, hd, :], bank[hd][:, 0:RELS], ACT.Copy).then_inc(rows_copied, 1)
            sc.wait_ge(norm_done, NORMS["mix"])
            split_x_hi(sc, "mix", mtmp)
            for j in range(4):
                ahead("c", j)
                computed(sc, "c", j)
                free(act_(cgate[:, 2 * j:2 * j + 2, :], unit_bank(U0["c"] + j)[:, :], ACT.Copy),
                     U0["c"] + j)
            for name in ("xc", "b"):
                for j in range(4):
                    ahead(name, j)
            sc.wait_ge(rows_stored, 16)
            for j in range(12):
                ahead("q", j)
                computed(sc, "q", j)
                free(act_(qk[:, 2 * j:2 * j + 2, :], unit_bank(U0["q"] + j)[:, :], ACT.Copy),
                     U0["q"] + j)
            for j in range(6):
                ahead("v", j)
                computed(sc, "v", j)
                for tt in range(TT):
                    ins = act_(v1[:, tt, j * T:(j + 1) * T], rows_bank(U0["v"] + j, tt)[:, 0:T], ACT.Copy)
                free(ins, U0["v"] + j)
            for name, dst, b0 in (("gc", sig_c, 0), ("ga", sig_a, 8)):
                for j in range(4):
                    ahead(name, j)
                    computed(sc, name, j)
                    for n in range(2):
                        ins = act_(dst[:, 2 * j + n, :], unit_bank(U0[name] + j)[:, n * T:(n + 1) * T],
                                   ACT.Sigmoid, bias=V("gate_bias", b0 + 2 * j + n))
                    free(ins, U0[name] + j)
            for j in range(1, 4):
                evacuated(sc, U0["b"] + j)
            split_x_hi(sc, "conv", conv)
            for j in range(4):
                ahead("conv_out", j)

            n1 = HEADS * TT

            def nblocks(i):
                return GROUPS * (i % 2 + 1)

            def exp1(i):
                n = (i % 2 + 1) * P
                sc.wait_ge(max_ready, i + 1)
                if i >= 2:
                    sc.wait_ge(t_ready, i - 1)
                act_(pr1[:, i % 2, :, 0:n], sc1[:, i % 2, :, 0:n], ACT.Exp,
                     bias=neg_max[:, i % 2:i % 2 + 1], accum_out=denom[:, i % 2:i % 2 + 1])\
                    .then_inc(exp_done, 1)

            def copy_t1(i):
                tb = [(0, 1), (2, 7)][i % 2]
                sc.wait_ge(t_ready, i + 1)
                if i >= 2:
                    sc.wait_ge(pv_done, i - 1)
                n = nblocks(i)
                ins = act_(pt1[:, i % 2, 0:min(n, 4) * P], bank[tb[0]][:, 0:min(n, 4) * P], ACT.Copy)
                if n > 4:
                    ins = act_(pt1[:, i % 2, 4 * P:n * P], bank[tb[1]][:, 0:(n - 4) * P], ACT.Copy)
                ins.then_inc(pt_ready, 1)

            def out1(i):
                hd, qt = i // 2, i % 2
                row = hd % 2 * HD
                sc.wait_ge(pv_done, i + 1)
                act_(o_t[row:row + HD, hd // 2, qt * P:(qt + 1) * P],
                     bank[[1, 7][i % 2]][row:row + HD, T:T + P], ACT.Copy).then_inc(o_done, 1)

            for i in range(n1 + 2):
                if i < n1:
                    exp1(i)
                if 1 <= i <= n1:
                    copy_t1(i - 1)
                if i >= 2:
                    out1(i - 2)

            sc.wait_ge(o_done, n1)
            computed(sc, "conv_out", 3)
            split_x_hi(sc, "attn", o_t, kt=4)
            for j in range(4):
                ahead("attn_out", j)
            for j in range(1, 4):
                evacuated(sc, U0["attn_out"] + j)
            split_x_hi(sc, "merged", merged)
            for j in range(4):
                ahead("w_out", j)
            sc.wait_ge(res_done, RES["mixer"])
            square(h[:, :, :], sq1)
            sqrt_mean(STATS["ffn"], 0)
            sc.wait_ge(norm_done, NORMS["ffn"])
            split_x_hi(sc, "ffn", mtmp)
            for j in range(8):
                ahead("wq", j)
                computed(sc, "wq", j)
                free(act_(pq[:, 2 * j:2 * j + 2, :], unit_bank(U0["wq"] + j)[:, :], ACT.Copy),
                     U0["wq"] + j)
            for j in range(8):
                sc.wait_ge(key_s, j + 1)
                free(act_(score[:, j // 4, j % 4 * 4:j % 4 * 4 + 4, :],
                          unit_bank(U0["keyscore"] + j)[:, :], ACT.Copy), U0["keyscore"] + j)

            def gelu(j, turns=0):
                ahead("down", j, turns)
                unit = U0["down"] + j
                sc.wait_ge(half_done, turns * 6 + 2 * (C0["down"] + j + 1))
                dst = act[:, bass.ds(turns * 6 + 2 * j, 2), :]
                free(act_(dst, unit_bank(unit)[:, :].rearrange("p (a b) -> p a b", a=2), ACT.Gelu), unit)

            with sc.Fori(0, 13) as it:
                for j in range(3):
                    gelu(j, it)
            sc.wait_ge(best_ready, 1)
            for tt in range(TT):
                act_(best[:, tt], best[:, tt], ACT.Exp).then_inc(best_exp, 1)
            with sc.Fori(13, TILES_BEFORE // 6) as it:
                for j in range(3):
                    gelu(j, it)
            sc.wait_ge(slots_copied, 1)
            with sc.Fori(TILES_BEFORE // 6, 21) as it:
                for j in range(3):
                    gelu(j, it)
            gelu(63)

            def split_act(j, turns=0):
                if isinstance(turns, int) and j + 3 * turns < 3:
                    pass
                else:
                    sc.wait_ge(half_done, turns * 6 + 2 * (C0["up"] + j - 2))
                at = 2 * j % 6
                act_(xh[:, at:at + 2, :], act[:, bass.ds(turns * 6 + 2 * j, 2), :], ACT.Copy)\
                    .then_inc(ah_ready, 1)

            with sc.Fori(0, T // 8) as it:
                for half in range(2):
                    b = onehots(half)[1]
                    sc.wait_ge(keys_matched[1][half], it + 1)
                    for tk in range(4):
                        act_(b[:, tk, :], b[:, tk, :], ACT.Copy,
                             scale=slot_t[:, 2, bass.ds(it * 8 + (half * 4 + tk), 1)])\
                            .then_inc(weighted[half], 1)
            for half in range(2):
                sc.wait_ge(gated[half], T // 8 + 1)
            for j in range(2):
                split_act(j)
            ahead("up", 0)
            split_act(2)
            ahead("up", 1)
            with sc.Fori(0, 20) as it:
                for j in range(2, 5):
                    split_act(j + 1, it)
                    ahead("up", j, it)
            split_act(63)
            ahead("up", 62)
            ahead("up", 63)

            for x in range(4):
                split_hi(sc, TWO + x)
            sc.wait_ge(res_done, RES["experts"])
            square(h[:, :, :], sq2)
            sqrt_mean(STATS["final"], 0)
            sc.wait_ge(norm_done, NORMS["final"])
            split_x_hi(sc, "final", h)
            sc.wait_ge(lam_sum, 1)
            act_(lam[:, 0:2], lam[:, 2:4], ACT.Exp).then_inc(lam_exp, 1)
            def diagonals(n0, n1):
                for n in range(n0, min(n1, DT * PE_TAPS)):
                    if n >= DIAGS:
                        sc.wait_ge(diag_used, n - DIAGS + 1)
                    act_(diag[:, n % DIAGS, :], ident, ACT.Copy,
                         scale=V("w_dw", n % PE_TAPS * 8 + n // PE_TAPS)).then_inc(diag_made, 1)

            diagonals(0, DIAGS)
            for j in range(8):
                ahead("pw1", j)
                computed(sc, "pw1", j)
                if j >= 2:
                    evacuated(sc, U0["pw1"] + j - 2)
                act_(sg2[:, j % 2, :], unit_bank(U0["pw1"] + j)[:, T:HALF], ACT.Sigmoid,
                     bias=V("b_pw1", 8 + j)).then_inc(glu_sig, 1)
                if j >= 2:
                    diagonals(DIAGS + (j - 2) * PE_TAPS,
                              DIAGS + (j - 1) * PE_TAPS if j < 7 else DT * PE_TAPS)

            def layer_norm(name, g, b, g0, dst, func=ACT.Identity):
                n = LNS[name]
                for q in range(4):
                    sc.wait_ge(centred, 4 * (n - 1) + q + 1)
                    act_(sq2[:, 2 * q:2 * q + 2, :], cen[:, 2 * q:2 * q + 2, :], ACT.Square)\
                        .then_inc(squared, 1)
                sqrt_mean(STATS[name] + 1, 1)
                for k in range(DT):
                    if k % 2 == 0:
                        sc.wait_ge(scaled, 4 * (n - 1) + k // 2 + 1)
                    ins = act_(dst[:, k, :], nrm[:, k, :], func, bias=V(b, g0 + k),
                               scale=V(g, g0 + k))
                ins.then_inc(norm_done, 1)

            layer_norm("conv", "ln_g", "ln_b", 0, cen, ACT.Silu)
            sc.wait_ge(norm_done, NORMS["conv"])
            split_x_hi(sc, "silu", cen)
            for j in range(4):
                ahead("pw2", j)
                computed(sc, "pw2", j)
                for n in range(2):
                    ins = act_(sq2[:, 2 * j + n, :],
                               unit_bank(U0["pw2"] + j)[:, n * T:(n + 1) * T], ACT.Identity,
                               bias=V("b_pw2", 2 * j + n))
                free(ins, U0["pw2"] + j)

            def gated_(layer, p, e, at):
                x0, n = 2 * C0[f"moe{layer}"] + 4, (p + 5 * layer) * 4 + 1 + e
                sc.wait_ge(half_done, p * PASS + (x0 + at))
                sc.wait_ge(hid32, n)
                act_(silu, bank[0][:, :], ACT.Silu).then_inc(silu_done, 1)

            def first_gate(layer, p):
                x0 = 2 * C0[f"moe{layer}"]
                for x in range(0 if p else 4, 8):
                    split_hi(sc, x0 + x, p, PASS)
                gated_(layer, p, 0, 0)

            def one_pass(layer, p, more, last_pass=False):
                x0, q = 2 * C0[f"moe{layer}"] + 4, p + 5 * layer
                n0 = q * 4 + 1

                def split(j):
                    for x in (2 * j + 4, 2 * j + 5):
                        if more or x < PASS - 4:
                            split_hi(sc, x0 + x, p, PASS)

                def flipped(e):
                    sc.wait_ge(t_done, n0 + e)
                    act_(hid_h, bank[2][:, :], ACT.Copy).then_inc(hid_hi, 1)

                split(0)
                split(1)
                for e in range(1, 4):
                    split(6 * e - 4)
                    split(6 * e - 3)
                    gated_(layer, p, e, 12 * e - 4)
                    if e == 1:
                        flipped(0)
                    split(6 * e - 2)
                    split(6 * e - 1)
                    if e == 3 and more:
                        sc.wait_ge(half_done, p * PASS + (x0 + 36))
                        act_(xh[:, :, 0:P], gxh[:, :, bass.ds(p * P + P, P)], ACT.Copy)\
                            .then_inc(xg_hi, 1)
                    split(6 * e)
                    split(6 * e + 1)
                    flipped(e)
                split(20)
                split(21)
                if more:
                    gated_(layer, p, 4, 44)
                    split(22)
                    split(23)
                sc.wait_ge(half_done, p * PASS + (x0 + (PASS if more else PASS - 4)))
                if last_pass:
                    sc.wait_ge(y_cleared, 2 * (layer + 1))
                for c in range(2):
                    ins = act_(yh[:, bass.ds(p, 1), c * HALF:(c + 1) * HALF].squeeze(1), bank[4 + c][:, :],
                               ACT.Copy)
                ins.then_inc(y_hi, 1)

            def experts(layer):
                for x in range(4):
                    split_hi(sc, 2 * C0[f"moe{layer}"] + x)
                sc.wait_ge(logits, layer + 1)
                act_(aff, bank[3][:, 0:TT * NE], ACT.Sigmoid).then_inc(affin, 1)
                for i in range(4):
                    sc.wait_ge(xt_t, 4 * layer + i + 1)
                    act_(xth[:, i // 2, i % 2 * HALF:(i % 2 + 1) * HALF], bank[4 + i][:, :], ACT.Copy)\
                        .then_inc(xt_hi, 1)
                for k in range(DT):
                    b_ = [(4, 5, 6), (7, 0, 1)][k % 2]
                    sc.wait_ge(gat_ready, DT * layer + k + 1)
                    act_(gxh[:, k, 0:4 * P], bank[b_[0]][:, :], ACT.Copy)
                    act_(gxh[:, k, 4 * P:5 * P], bank[b_[2]][:, 0:P], ACT.Copy)
                    act_(gxl[:, k, 4 * P:5 * P], bank[b_[2]][:, P:2 * P], ACT.Copy).then_inc(gat_hi, 1)
                sc.wait_ge(gat_hi, DT * (layer + 1))
                act_(xh[:, :, 0:P], gxh[:, :, 0:P], ACT.Copy).then_inc(xg_hi, 1)
                first_gate(layer, 0)
                with sc.Fori(0, 3) as p:
                    one_pass(layer, p, True)
                one_pass(layer, 3, False)
                fifth = sc.value_load(flags[0:1, 0:1], min_val=0, max_val=1)
                with sc.If(fifth > 0):
                    sc.wait_ge(half_done, 2 * C0[f"moe{layer}"] + 4 * PASS)
                    act_(xh[:, :, 0:P], gxh[:, :, 4 * P:5 * P], ACT.Copy).then_inc(xg_hi, 1)
                    first_gate(layer, 4)
                    one_pass(layer, 4, False, True)
                with sc.Else():
                    sc.wait_ge(y_hi, 5 * layer + 5)
                    sc.sem_inc(hi_ready, PASS)
                    sc.sem_inc(silu_done, 4)
                    sc.sem_inc(hid_hi, 4)
                    sc.sem_inc(y_hi, 1)
                    sc.sem_inc(xg_hi, 1)

            layer_norm("mix0", "ln_mix_g", "ln_mix_b", 0, h)
            experts(0)
            layer_norm("ffn0", "ln_ffn_g", "ln_ffn_b", 0, h)
            sc.wait_ge(norm_done, NORMS["ffn0"])
            split_x_hi(sc, "kvq", h)
            for x in range(4):
                split_hi(sc, 2 * C0["k2"] + x)
            for name, dst in (("k2", k2), ("v2", None), ("q2", q2)):
                for j in range(4):
                    ahead(name, j)
                    computed(sc, name, j)
                    if dst is None:
                        for tt in range(TT):
                            ins = act_(v2[:, tt, j * T:(j + 1) * T], rows_bank(U0[name] + j, tt)[:, 0:T],
                                       ACT.Copy)
                    else:
                        ins = act_(dst[:, 2 * j:2 * j + 2, :], unit_bank(U0[name] + j)[:, :], ACT.Copy)
                    free(ins, U0[name] + j)

            def exp2(i):
                n = (i % 2 + 1) * P
                sc.wait_ge(max_ready, n1 + i + 1)
                if i >= 2:
                    sc.wait_ge(t_ready, n1 + i - 1)
                for c in range(2):
                    ins = act_(pr2[:, i % 2, c, 0:n], sc2[:, i % 2, c, 0:n], ACT.Exp,
                               bias=neg_max[:, i % 2 * 2 + c:i % 2 * 2 + c + 1],
                               accum_out=denom[:, i % 2 * 2 + c:i % 2 * 2 + c + 1])
                ins.then_inc(exp_done, 1)

            def copy_t2(i):
                n = (i % 2 + 1) * P
                sc.wait_ge(t_ready, n1 + i + 1)
                if i >= 2:
                    sc.wait_ge(pv_done, n1 + i - 1)
                act_(pt2[:, i % 2, 0:n], bank[5 + i % 2][:, 0:n], ACT.Copy).then_inc(pt_ready, 1)

            def out2(i):
                hd, qt = i // 2, i % 2
                sc.wait_ge(pv_done, n1 + i + 1)
                src = bank[5 + i % 2][:, T:T + P]
                own(act_(sq2[:, i % 2, 0:P], src, ACT.Square, scale=rden2[:, i, 0:1],
                         accum_out=sumsq[:, i:i + 1]))
                act_(o_rows(qt)[:, hd * P:(hd + 1) * P], src, ACT.Copy,
                     scale=rden2[:, i, 0:1]).then_inc(o_done, 1)

            for i in range(n1 + 2):
                if i < n1:
                    exp2(i)
                if 1 <= i <= n1:
                    copy_t2(i - 1)
                if i >= 2:
                    out2(i - 2)
            sc.wait_ge(o_done, 2 * n1)
            act_(sumsq, sumsq, ACT.Sqrt, bias=eps[:, 1:2], scale=1.0 / P).then_inc(sub_root, 1)
            for n in range(4):
                sc.wait_ge(sub_t, n + 1)
                act_(at_out[:, 2 * n:2 * n + 2, :], bank[n][:, :], ACT.Copy,
                     scale=sub_g).then_inc(sub_out, 1)
            sc.wait_ge(sub_out, 4)
            split_x_hi(sc, "at_out", at_out)
            for j in range(4):
                ahead("w_o", j)
            layer_norm("mix1", "ln_mix_g", "ln_mix_b", 8, h)
            experts(1)
            layer_norm("ffn1", "ln_ffn_g", "ln_ffn_b", 8, h)

        @block.vector
        def _(ve):
            step = [0]
            vx = nc.vector

            def own(ins):
                step[0] += 1
                ins.then_inc(dve_step, 1)
                ve.wait_ge(dve_step, step[0])

            def free(ins, unit):
                ins.then_inc(unit_free[unit % UNIT_BANKS], 1)

            def pair(ap):
                return ap.rearrange("p (a b) -> p a b", a=2)

            def ahead(name, j, turns=0):
                for x in halves_ahead(name, j):
                    split_lo(ve, x, turns)

            def rms_apply(name, vname, dst):
                ve.wait_ge(root_ready, ROOTS[name])
                own(vx.reciprocal(root[:, :], root[:, :]))
                for k in range(DT):
                    ins = vx.scalar_tensor_tensor(dst[:, k, :], h[:, k, :], V(vname, k), root[:, :],
                                                  ALU.mult, ALU.mult)
                ins.then_inc(norm_done, 1)

            ve.sem_inc(hid32, 1)
            ve.sem_inc(hid_done, 1)
            ve.sem_inc(y_done, 1)
            ve.wait_ge(loaded, 9 * 16)
            own(vx.tensor_copy(turn, ang.bitcast(I32)))
            own(vx.tensor_scalar(ang, turn, C("freq"), None, ALU.mult))
            magic = 1.5 * 2.0 ** 23
            own(vx.tensor_scalar(turn, ang, 1.0 / (2 * math.pi), magic, ALU.mult, ALU.add))
            own(vx.tensor_scalar(turn, turn, magic, None, ALU.subtract))
            c1 = 6.28125
            c2 = float(np.float32(np.round((2 * math.pi - c1) * 2 ** 20) / 2 ** 20))
            c3 = 2 * math.pi - c1 - c2
            for c in (c1, c2, c3):
                own(vx.scalar_tensor_tensor(ang, turn, -c, ang, ALU.mult, ALU.add))
            vx.tensor_scalar(ang, ang, 3.1415925, -3.1415925, ALU.min, ALU.max)\
                .then_inc(angles_ready, 1)
            split_lo(ve, 0)
            split_lo(ve, 1)
            rms_apply("mix", "norm_mix", mtmp)
            ve.wait_ge(rope_ready, 2)
            own(vx.tensor_tensor(cos_t, cos_t, cos_t, ALU.mult))
            own(vx.tensor_scalar(cos_t, cos_t, -2.0, 1.0, ALU.mult, ALU.add))
            split_x_lo(ve, "mix", mtmp)
            for j in range(4):
                ahead("c", j)

            ve.wait_ge(set_up, 6)
            for j in range(4):
                ahead("xc", j)
                computed(ve, "xc", j)
                evacuated(ve, U0["c"] + j)
                free(vx.tensor_tensor(z[:, 2 * j:2 * j + 2, 2:T + 2], cgate[:, 2 * j:2 * j + 2, :],
                                      pair(unit_bank(U0["xc"] + j)[:, :]), ALU.mult), U0["xc"] + j)
            for j in range(4):
                evacuated(ve, U0["xc"] + j)
            for i in range(3):
                ahead("b", i)
                for k in range(DT):
                    src = z[:, k, i:i + T]
                    if i == 0:
                        ins = vx.tensor_scalar(conv[:, k, :], src, V("conv_w", k), None, ALU.mult)
                    else:
                        ins = vx.scalar_tensor_tensor(conv[:, k, :], src, V("conv_w", i * 8 + k),
                                                      conv[:, k, :], ALU.mult, ALU.add)
                own(ins)
            for j in range(4):
                if j == 1:
                    ahead("b", 3)
                computed(ve, "b", j)
                free(vx.tensor_tensor(conv[:, 2 * j:2 * j + 2, :], conv[:, 2 * j:2 * j + 2, :],
                                      pair(unit_bank(U0["b"] + j)[:, :]), ALU.mult), U0["b"] + j)
            ahead("q", 0)
            for j in range(12):
                ahead("q", j + 1)
                ve.wait_ge(rot_ready, j + 1)
                t = qk[:, 2 * j:2 * j + 2, :]
                vx.tensor_tensor(rot_tmp, pair(bank[3 + j % 2][:, :]),
                                 sin_t.unsqueeze(1).broadcast_to([P, 2, T]), ALU.mult)
                own(vx.tensor_tensor(t, t, cos_t.unsqueeze(1).broadcast_to([P, 2, T]), ALU.mult))
                vx.tensor_tensor(t, t, rot_tmp, ALU.add).then_inc(rot_done, 1)
                ve.wait_ge(rot_done, j + 1)
            for j in range(1, 6):
                ahead("v", j)
            for name in ("gc", "ga"):
                for j in range(4):
                    ahead(name, j)
            split_x_lo(ve, "conv", conv)
            for j in range(4):
                ahead("conv_out", j)
                computed(ve, "conv_out", j)
                evacuated(ve, U0["gc"] + j)
                free(vx.tensor_tensor(merged[:, 2 * j:2 * j + 2, :], sig_c[:, 2 * j:2 * j + 2, :],
                                      pair(unit_bank(U0["conv_out"] + j)[:, :]), ALU.mult),
                     U0["conv_out"] + j)

            n1 = HEADS * TT

            def masked(i):
                qt, s = i % 2, i % 2
                n = (qt + 1) * P
                ve.wait_ge(s_ready, i + 1)
                if i >= 2:
                    ve.wait_ge(exp_done, i - 1)
                b0, b1 = bank[3 + s * 2], bank[4 + s * 2]
                vx.scalar_tensor_tensor(sc1[:, s, 0:2, 0:n], pair(b0[:, :])[:, :, 0:n], HD ** -0.5,
                                        mask[:, 0:2, (1 - qt) * P:(1 - qt) * P + n],
                                        ALU.mult, ALU.add)
                vx.scalar_tensor_tensor(sc1[:, s, 2, 0:n], b1[:, 0:n], HD ** -0.5,
                                        mask[:, 2, (1 - qt) * P:(1 - qt) * P + n],
                                        ALU.mult, ALU.add).then_inc(s_read, 1)
                ve.wait_ge(s_read, i + 1)
                vx.tensor_reduce(neg_max[:, s:s + 1], sc1[:, s, :, 0:n], AX.XY, ALU.max,
                                 negate=True).then_inc(max_ready, 1)

            def normal(i):
                s, n = i % 2, (i % 2 + 1) * P
                ve.wait_ge(exp_done, i + 1)
                own(vx.reciprocal(rden[:, s:s + 1], denom[:, s:s + 1]))
                vx.tensor_scalar(pr1[:, s, :, 0:n], pr1[:, s, :, 0:n], rden[:, s:s + 1], None,
                                 ALU.mult).then_inc(p_ready, 1)

            masked(0)
            for i in range(n1):
                if i + 1 < n1:
                    masked(i + 1)
                normal(i)

            split_x_lo(ve, "attn", o_t, kt=4)
            for j in range(4):
                ahead("attn_out", j)
                computed(ve, "attn_out", j)
                evacuated(ve, U0["ga"] + j)
                src = pair(unit_bank(U0["attn_out"] + j)[:, :])
                m = merged[:, 2 * j:2 * j + 2, :]
                own(vx.tensor_tensor(rot_tmp, sig_a[:, 2 * j:2 * j + 2, :], src, ALU.mult))
                free(vx.tensor_tensor(m, m, rot_tmp, ALU.add), U0["attn_out"] + j)
                evacuated(ve, U0["attn_out"] + j)
            split_x_lo(ve, "merged", merged)
            for j in range(4):
                ahead("w_out", j)
                computed(ve, "w_out", j)
                hh = h[:, 2 * j:2 * j + 2, :]
                free(vx.tensor_tensor(hh, hh, pair(unit_bank(U0["w_out"] + j)[:, :]), ALU.add),
                     U0["w_out"] + j)
            own(vx.memset(neg_max, 0.0))
            vx.memset(denom, 0.0).then_inc(res_done, 1)
            rms_apply("ffn", "norm_ffn", mtmp)
            split_x_lo(ve, "ffn", mtmp)
            for j in range(8):
                ahead("wq", j)

            for j in range(8):
                evacuated(ve, U0["keyscore"] + j)
            def routing():
                both = [(tt, c) for tt in range(TT) for c in range(2 * PH)]
                ti = top_i.bitcast(U32)

                def best_of(pairs, values, out, out_i, cost):
                    for lo in (0, 8):
                        for x in pairs:
                            ins = vx.max(out(*x)[:, lo:lo + 8], values(*x))
                            yield cost
                        own(ins)
                        for x in pairs:
                            ins = vx.max_index(out_i(*x)[:, lo:lo + 8], out(*x)[:, lo:lo + 8], values(*x))
                            yield cost
                        own(ins)
                        if lo == 0:
                            for x in pairs:
                                ins = vx.match_replace(values(*x), out(*x)[:, 0:8], values(*x), -3e38)
                                yield cost
                            own(ins)

                yield from best_of(both, lambda tt, c: score[:, tt, c, :],
                                   lambda tt, c: top_v[:, tt, c, :], lambda tt, c: ti[:, tt, c, :], 1)
                own(vx.tensor_copy(top_f, ti))
                bi = best_i.bitcast(U32)
                for tt in range(TT):
                    for hd in range(PH):
                        ins = vx.tensor_tensor(
                            cand[:, hd, :].rearrange("p (a b) -> p a b", a=TOPK),
                            top_v[:, tt, 2 * hd, :].unsqueeze(2).broadcast_to([P, TOPK, TOPK]),
                            top_v[:, tt, 2 * hd + 1, :].unsqueeze(1).broadcast_to([P, TOPK, TOPK]),
                            ALU.add)
                        yield WIDE_STEP
                    own(ins)
                    yield from best_of([(hd,) for hd in range(PH)], lambda hd: cand[:, hd, :],
                                       lambda hd: best[:, tt, hd, :], lambda hd: bi[:, tt, hd, :], WIDE_STEP)
                for tt in range(TT):
                    own(vx.tensor_copy(slot[:, 2, tt, 0:PH], best[:, tt, :, 0]))
                    ins = vx.tensor_tensor(best[:, tt], best[:, tt],
                                           slot[:, 2, tt, 0:PH].unsqueeze(2).broadcast_to([P, PH, TOPK]),
                                           ALU.subtract)
                    if tt == 0:
                        own(ins)
                ins.then_inc(best_ready, 1)
                yield WIDE_STEP
                bi_flat = bi.rearrange("p a b c -> p a (b c)")
                pa, pb = pos_a.bitcast(U32), pos_b.bitcast(U32)
                vx.tensor_scalar(pa, bi_flat, 4, None, ALU.logical_shift_right)
                own(vx.tensor_scalar(pb, bi_flat, TOPK - 1, None, ALU.bitwise_and))
                vx.tensor_copy(pos_f[:, 0], pa)
                own(vx.tensor_copy(pos_f[:, 1], pb))
                yield MATCH_STEP
                iota = C("iota")[:, 0:TOPK]
                for tt in range(TT):
                    for half in range(2):
                        for hd in range(PH):
                            ins = vx.tensor_tensor(
                                match[:, hd],
                                pos_f[:, half, tt, hd * TOPK:(hd + 1) * TOPK].unsqueeze(2)
                                .broadcast_to([P, TOPK, TOPK]),
                                iota.unsqueeze(1).broadcast_to([P, TOPK, TOPK]), ALU.is_equal)
                            yield MATCH_STEP
                        own(ins)
                        for hd in range(PH):
                            ins = vx.tensor_tensor(
                                match[:, hd], match[:, hd],
                                top_f[:, tt, 2 * hd + half, :].unsqueeze(1)
                                .broadcast_to([P, TOPK, TOPK]), ALU.mult)
                            yield MATCH_STEP
                        own(ins)
                        own(vx.tensor_reduce(slot[:, half, tt, :].rearrange("p (a b) -> p a b", a=PH),
                                             match, AX.X, ALU.add))
                        yield 3 * MATCH_STEP
                for tt in range(TT):
                    ve.wait_ge(best_exp, tt + 1)
                    own(vx.tensor_reduce(gsum[:, tt, :], best[:, tt], AX.X, ALU.add))
                    own(vx.reciprocal(gsum[:, tt, :], gsum[:, tt, :]))
                    ins = vx.tensor_tensor(slot[:, 2, tt, :].rearrange("p (a b) -> p a b", a=PH),
                                           best[:, tt],
                                           gsum[:, tt, :].unsqueeze(2).broadcast_to([P, PH, TOPK]),
                                           ALU.mult)
                    if tt == 0:
                        own(ins)
                ins.then_inc(slots_ready, 1)

            steps, due = routing(), 0
            for j in range(TILES_BEFORE // 2):
                ahead("down", j)
                due += ROUTING_STEPS
                while due > 0:
                    due -= next(steps, due)
            assert next(steps, "end") == "end"
            ve.wait_ge(slots_t, 1)
            for n in range(3):
                vx.tensor_copy(slot_t[:, n, :], bank[4 + n][:, 0:T])\
                    .then_inc([gated[0], gated[1], slots_copied][n], 1)
            with ve.Fori(TILES_BEFORE // 6, 21) as it:
                for j in range(3):
                    ahead("down", j, it)
            ahead("down", 63)
            computed(ve, "down", 63)
            ve.wait_ge(slots_copied, 1)
            for unit in range(U0["pw1"] - 3, U0["pw1"]):
                evacuated(ve, unit)

            def match_keys(it, half):
                ve.wait_ge(scattered[half], it + 1)
                for c in (1, 0):
                    vx.tensor_tensor(onehots(half)[c], C("iota").unsqueeze(1).broadcast_to([P, 4, P]),
                                     slot_t[:, c, bass.ds(it * 8 + half * 4, 4)].unsqueeze(2)
                                     .broadcast_to([P, 4, P]),
                                     ALU.is_equal).then_inc(keys_matched[c][half], 1)

            def gate(it, half):
                ve.wait_ge(scattered[half], it + 2)
                a = act[:, :, bass.ds(it * 8 + half * 4, 4)]
                vx.tensor_tensor(a, a, bank[4 + half][:, :].rearrange("p (i t) -> p i t", t=4),
                                 ALU.mult).then_inc(gated[half], 1)

            match_keys(0, 0)
            with ve.Fori(0, T // 8 - 1) as it:
                match_keys(it, 1)
                gate(it, 0)
                match_keys(it + 1, 0)
                gate(it, 1)
            match_keys(T // 8 - 1, 1)
            gate(T // 8 - 1, 0)
            gate(T // 8 - 1, 1)

            def residual(done, scale):
                for b_ in range(4):
                    hh = h[:, 2 * b_:2 * b_ + 2, :]
                    if scale is None:
                        ins = vx.tensor_tensor(hh, hh, pair(bank[4 + b_][:, :]), ALU.add)
                    else:
                        ins = vx.scalar_tensor_tensor(pre[:, 2 * b_:2 * b_ + 2, :], hh, scale,
                                                      pair(bank[4 + b_][:, :]), ALU.mult, ALU.add)
                return ins

            for half in range(2):
                ve.wait_ge(gated[half], T // 8 + 1)

            def split_act(j, turns=0):
                ve.wait_ge(ah_ready, turns * 3 + j + 1)
                at = 2 * j % 6
                vx.tensor_tensor(xl[:, at:at + 2, :], act[:, bass.ds(turns * 6 + 2 * j, 2), :],
                                 xh[:, at:at + 2, :].bitcast(F32), ALU.subtract).then_inc(a_ready, 1)

            for j in range(2):
                split_act(j)
            ahead("up", 0)
            split_act(2)
            ahead("up", 1)
            with ve.Fori(0, 20) as it:
                for j in range(2, 5):
                    split_act(j + 1, it)
                    ahead("up", j, it)
            split_act(63)
            ahead("up", 62)
            ahead("up", 63)
            for x in range(4):
                split_lo(ve, TWO + x)
            computed(ve, "up", 63)
            residual(None, None).then_inc(res_done, 1)
            rms_apply("final", "final_norm", h)
            split_x_lo(ve, "final", h)

            ve.wait_ge(two_loaded, 2 * 16)
            own(vx.tensor_tensor(lamp[:, 1, 0:HD], lamp[:, 0, 0:HD], lamp[:, 0, HD:2 * HD], ALU.mult))
            own(vx.tensor_tensor(lamp[:, 1, HD:2 * HD], lamp[:, 0, 2 * HD:3 * HD],
                                 lamp[:, 0, 3 * HD:4 * HD], ALU.mult))
            vx.tensor_reduce(lam[:, 2:4], lamp[:, 1, 0:2 * HD].rearrange("p (a b) -> p a b", a=2),
                             AX.X, ALU.add).then_inc(lam_sum, 1)
            ve.wait_ge(lam_exp, 1)
            own(vx.tensor_tensor(lam[:, 2:3], lam[:, 1:2], lam[:, 0:1], ALU.subtract))
            own(vx.tensor_scalar(lam[:, 2:3], lam[:, 2:3], LAMBDA_INIT, None, ALU.subtract))
            own(vx.tensor_scalar(sub_g, V("subln_g", 0), 1.0 - LAMBDA_INIT, None, ALU.mult))
            own(vx.memset(glu[:, :, 0:TAPS - 1], 0.0))
            for j in range(8):
                ahead("pw1", j)
                ve.wait_ge(glu_sig, j + 1)
                free(vx.scalar_tensor_tensor(glu[:, j, TAPS - 1:TAPS - 1 + T],
                                             unit_bank(U0["pw1"] + j)[:, 0:T], V("b_pw1", j),
                                             sg2[:, j % 2, :], ALU.add, ALU.mult), U0["pw1"] + j)
                if j % 2 == 0:
                    continue
                evacuated(ve, U0["pw1"] + j - 1)
                evacuated(ve, U0["pw1"] + j)
                for k in (j - 1, j):
                    step[0] += 1
                    vx.tensor_scalar(pre[:, k, :], glu[:, k, PE_TAPS:PE_TAPS + T],
                                     V("w_dw", PE_TAPS * 8 + k), V("b_dw", k), ALU.mult, ALU.add).then_inc(dve_step, 1)
                for i in range(PE_TAPS + 1, TAPS):
                    for k in (j - 1, j):
                        step[0] += 1
                        ve.wait_ge(dve_step, step[0] - 2)
                        vx.scalar_tensor_tensor(pre[:, k, :], glu[:, k, i:i + T], V("w_dw", i * 8 + k),
                                                pre[:, k, :], ALU.mult, ALU.add).then_inc(dve_step, 1)
                ve.wait_ge(dve_step, step[0])
                ve.wait_ge(diag_used, (j + 1) * PE_TAPS)
                ins = vx.tensor_tensor(pre[:, j - 1:j + 1, :], pre[:, j - 1:j + 1, :],
                                       pair(bank[4 + j // 2][:, :]), ALU.add)
                if j < 7:
                    own(ins)
            ins.then_inc(stat_in, 1)

            def layer_norm(name):
                ve.wait_ge(stat_out, STATS[name])
                wide = [P, 2, T]
                for q in range(4):
                    at = slice(2 * q, 2 * q + 2)
                    vx.tensor_tensor(cen[:, at, :], pre[:, at, :],
                                     bank[3][:, 0:T].unsqueeze(1).broadcast_to(wide),
                                     ALU.subtract).then_inc(centred, 1)
                ve.wait_ge(root_ready, ROOTS[name])
                own(vx.reciprocal(root[:, :], root[:, :]))
                for q in range(4):
                    at = slice(2 * q, 2 * q + 2)
                    vx.tensor_tensor(nrm[:, at, :], cen[:, at, :],
                                     root[:, :].unsqueeze(1).broadcast_to(wide),
                                     ALU.mult).then_inc(scaled, 1)

            layer_norm("conv")
            split_x_lo(ve, "silu", cen)
            for j in range(4):
                ahead("pw2", j)
                evacuated(ve, U0["pw2"] + j)
                ins = vx.scalar_tensor_tensor(pre[:, 2 * j:2 * j + 2, :], h[:, 2 * j:2 * j + 2, :], ALPHA,
                                              sq2[:, 2 * j:2 * j + 2, :], ALU.mult, ALU.add)
            ins.then_inc(stat_in, 1)
            layer_norm("mix0")

            def experts(layer):
                for x in range(4):
                    split_lo(ve, 2 * C0[f"moe{layer}"] + x)
                ve.wait_ge(affin, layer + 1)
                own(vx.tensor_tensor(sel, aff, rbias[:, :].unsqueeze(1).broadcast_to([P, TT, NE]), ALU.add))
                low = C("lower").rearrange("p (a b) -> p a b", a=EPG)
                big4 = hid[:, 0:128]
                big4b = hid[:, 128:256]

                def ranks(values, out, n):
                    v4 = values.rearrange("p (n e) -> p n e", e=EPG)
                    for g in range(n):
                        other = v4[:, g, :].unsqueeze(1).broadcast_to([P, EPG, EPG])
                        mine = v4[:, g, :].unsqueeze(2).broadcast_to([P, EPG, EPG])
                        a = big4[:, g * 16:(g + 1) * 16].rearrange("p (a b) -> p a b", a=EPG)
                        b = big4b[:, g * 16:(g + 1) * 16].rearrange("p (a b) -> p a b", a=EPG)
                        vx.tensor_tensor(a, other, mine, ALU.is_gt)
                        ins = vx.tensor_tensor(b, other, mine, ALU.is_equal)
                    own(ins)
                    m = n * 16
                    bb = big4b[:, 0:m].rearrange("p (n m) -> p n m", m=16)
                    own(vx.tensor_tensor(bb, bb, C("lower").unsqueeze(1).broadcast_to([P, n, 16]), ALU.mult))
                    own(vx.tensor_tensor(big4[:, 0:m], big4[:, 0:m], big4b[:, 0:m], ALU.add))
                    own(vx.tensor_reduce(out, big4[:, 0:m].rearrange("p (n m) -> p n m", m=EPG),
                                         AX.X, ALU.add))

                sel_f = sel.rearrange("p a b -> p (a b)")
                top2_f = top2.rearrange("p a b -> p (a b)")
                gsel_f = gsel.rearrange("p a b -> p (a b)")
                ranks(sel_f, rank, TT * NG)
                own(vx.tensor_scalar(top2_f, rank, 1.5, None, ALU.is_lt))
                own(vx.tensor_tensor(gsel_f, sel_f, top2_f, ALU.mult))
                own(vx.tensor_reduce(gscore, gsel_f.rearrange("p (n e) -> p n e", e=EPG), AX.X, ALU.add))
                ranks(gscore, grank, TT)
                vx.tensor_scalar(grank, grank, 0.5, None, ALU.is_lt).then_inc(groups_ready, 1)
                ve.wait_ge(groups_ready, layer + 1)
                own(vx.tensor_tensor(top2_f.rearrange("p (n e) -> p n e", e=EPG),
                                     top2_f.rearrange("p (n e) -> p n e", e=EPG),
                                     grank.unsqueeze(2).broadcast_to([P, TT * NG, EPG]), ALU.mult))
                own(vx.tensor_tensor(gates, aff, top2, ALU.mult))
                own(vx.tensor_reduce(wsum, gates, AX.X, ALU.add))
                own(vx.reciprocal(wsum, wsum))
                vx.tensor_tensor(gates, gates, wsum.unsqueeze(2).broadcast_to([P, TT, NE]), ALU.mult)\
                    .then_inc(gates_ready, 1)
                ve.wait_ge(places_ready, layer + 1)
                own(vx.tensor_scalar(over, bank[3][:, 40:44], P + 0.5, None, ALU.is_gt))
                own(vx.tensor_tensor(tmp8, bank[3][:, 32:40], grank, ALU.mult))
                own(vx.tensor_reduce(place, tmp8.rearrange("p (t g) -> p t g", g=NG), AX.X, ALU.add))
                own(vx.tensor_tensor(tmp8b, grank, C("base"), ALU.mult))
                own(vx.tensor_reduce(first, tmp8b.rearrange("p (t g) -> p t g", g=NG), AX.X, ALU.add))
                own(vx.tensor_scalar(fits, place, P - 0.5, None, ALU.is_lt))
                own(vx.tensor_scalar(first, first, 3.0 * P, None, ALU.subtract))
                own(vx.tensor_tensor(first, first, fits, ALU.mult))
                own(vx.tensor_tensor(slot_id, first, place, ALU.add))
                own(vx.tensor_scalar(slot_id, slot_id, 3.0 * P, None, ALU.add))
                if layer == 0:
                    ve.wait_ge(two_loaded, 2 * 16)
                for tt in range(TT):
                    vx.tensor_scalar(pick_t[:, tt, :], slot_no, slot_id[:, tt:tt + 1], None, ALU.is_equal)
                    ins = vx.tensor_scalar(silu[:, tt * P:(tt + 1) * P], ident, slot_id[:, tt:tt + 1], None,
                                           ALU.mult)
                ins.then_inc(slots_made, 1)
                for i in range(4):
                    ve.wait_ge(xt_hi, 4 * layer + i + 1)
                    at = slice(i % 2 * HALF, (i % 2 + 1) * HALF)
                    vx.tensor_tensor(xtl[:, i // 2, at], bank[4 + i][:, :],
                                     xth[:, i // 2, at].bitcast(F32), ALU.subtract).then_inc(xt_lo, 1)
                own(vx.tensor_tensor(over_i, over, C("index"), ALU.mult))
                own(vx.tensor_reduce(flag_f[:, 0:1], over, AX.X, ALU.add))
                own(vx.tensor_reduce(flag_f[:, 1:2], over_i, AX.X, ALU.add))
                vx.tensor_copy(flags[:, :], flag_f).then_inc(flags_ready, 1)
                ve.wait_ge(slot_row, layer + 1)
                for i in range(5):
                    ins = vx.tensor_scalar(pick_s[:, i, :], bank[3][:, T:2 * T], float(-i * P), C("row"),
                                           ALU.add, ALU.is_equal)
                ins.then_inc(picks_ready, 1)
                ve.wait_ge(sg_ready, layer + 1)
                own(vx.tensor_copy(slot_gate[:, :], bank[2][:, 0:5 * NE]))
                for k in range(DT):
                    b_ = [(4, 5, 6), (7, 0, 1)][k % 2]
                    ve.wait_ge(gat_ready, DT * layer + k + 1)
                    vx.tensor_copy(gxl[:, k, 0:4 * P], bank[b_[1]][:, :]).then_inc(gat_lo, 1)
                ve.wait_ge(gat_lo, DT * (layer + 1))
                ve.wait_ge(xg_hi, 5 * layer + 1)
                vx.tensor_copy(xl[:, :, 0:P], gxl[:, :, 0:P]).then_inc(xg_ready, 1)

                def first_gate(p):
                    for x in range(0 if p else 4, 8):
                        split_lo(ve, 2 * C0[f"moe{layer}"] + x, p, PASS)

                def one_pass(p, group, more, last_pass=False):
                    x0, q = 2 * C0[f"moe{layer}"] + 4, p + 5 * layer
                    n0 = q * 4 + 1

                    def split(j):
                        for x in (2 * j + 4, 2 * j + 5):
                            if more or x < PASS - 4:
                                split_lo(ve, x0 + x, p, PASS)

                    def hidden(e):
                        ve.wait_ge(half_done, p * PASS + (x0 + (12 * e if e else 4)))
                        ve.wait_ge(silu_done, n0 + e + 1)
                        if e >= 1:
                            ve.wait_ge(t_done, n0 + e - 1)
                        vx.scalar_tensor_tensor(hid, silu,
                                                slot_gate[:, bass.ds(p * NE + group * EPG + e, 1)],
                                                bank[1][:, :], ALU.mult, ALU.mult).then_inc(hid32, 1)

                    def flipped(e):
                        ve.wait_ge(hid_hi, n0 + e)
                        vx.tensor_tensor(hid_l, bank[2][:, :].rearrange("p (f s) -> p f s", f=4),
                                         hid_h.bitcast(F32), ALU.subtract).then_inc(hid_done, 1)

                    split(0)
                    split(1)
                    hidden(0)
                    for e in range(1, 4):
                        split(6 * e - 4)
                        split(6 * e - 3)
                        if e == 1:
                            flipped(0)
                        split(6 * e - 2)
                        split(6 * e - 1)
                        hidden(e)
                        if e == 3 and more:
                            ve.wait_ge(xg_hi, q + 2)
                            vx.tensor_copy(xl[:, :, 0:P], gxl[:, :, bass.ds(p * P + P, P)])\
                                .then_inc(xg_ready, 1)
                        split(6 * e)
                        split(6 * e + 1)
                        flipped(e)
                    for j in range(20, 24):
                        split(j)
                    ve.wait_ge(y_hi, q + 2)
                    if last_pass:
                        ve.wait_ge(y_cleared, 2 * (layer + 1))
                    for c in range(2):
                        at = slice(c * HALF, (c + 1) * HALF)
                        ins = vx.tensor_tensor(yl[:, bass.ds(p, 1), at].squeeze(1), bank[4 + c][:, :],
                                               yh[:, bass.ds(p, 1), at].squeeze(1).bitcast(F32), ALU.subtract)
                    ins.then_inc(y_done, 1)

                first_gate(0)
                with ve.Fori(0, 3) as p:
                    one_pass(p, p, True)
                one_pass(3, 3, False)
                fifth = ve.value_load(flags[0:1, 0:1], min_val=0, max_val=1)
                group = ve.value_load(flags[0:1, 1:2], min_val=0, max_val=NG - 1)
                with ve.If(fifth > 0):
                    ve.wait_ge(xg_hi, 5 * layer + 5)
                    vx.tensor_copy(xl[:, :, 0:P], gxl[:, :, 4 * P:5 * P]).then_inc(xg_ready, 1)
                    first_gate(4)
                    one_pass(4, group, False, True)
                with ve.Else():
                    ve.wait_ge(y_done, 5 * layer + 5)
                    ve.sem_inc(lo_ready, PASS)
                    ve.sem_inc(hid32, 4)
                    ve.sem_inc(hid_done, 4)
                    ve.sem_inc(y_done, 1)
                    ve.sem_inc(xg_ready, 1)
                for n in range(4):
                    ve.wait_ge(back, 4 * layer + n + 1)
                    at = slice(2 * n, 2 * n + 2)
                    ins = vx.scalar_tensor_tensor(pre[:, at, :], h[:, at, :], ALPHA,
                                                  pair(bank[[6, 7, 0, 1][n]][:, :]), ALU.mult, ALU.add)
                ins.then_inc(stat_in, 1)

            experts(0)
            layer_norm("ffn0")
            split_x_lo(ve, "kvq", h)
            for x in range(4):
                split_lo(ve, 2 * C0["k2"] + x)
            for name in ("k2", "v2", "q2"):
                for j in range(4):
                    ahead(name, j)

            ve.wait_ge(rel_loaded, HEADS * 16)

            def biased(i):
                hd, qt, s = i // 2, i % 2, i % 2
                n = (qt + 1) * P
                ve.wait_ge(s_ready, n1 + i + 1)
                if i >= 2:
                    ve.wait_ge(exp_done, n1 + i - 1)
                rel = relb[:, hd, (1 - qt) * P:(1 - qt) * P + n]
                vx.scalar_tensor_tensor(sc2[:, s, :, 0:n], pair(bank[3 + s][:, :])[:, :, 0:n], HD ** -0.5,
                                        rel.unsqueeze(1).broadcast_to([P, 2, n]), ALU.mult, ALU.add)\
                    .then_inc(s_read, 1)
                ve.wait_ge(s_read, n1 + i + 1)
                vx.tensor_reduce(neg_max[:, 2 * s:2 * s + 2], sc2[:, s, :, 0:n], AX.X, ALU.max,
                                 negate=True).then_inc(max_ready, 1)

            def difference(i):
                s, n = i % 2, (i % 2 + 1) * P
                ve.wait_ge(exp_done, n1 + i + 1)
                r = rden2[:, i, :]
                own(vx.reciprocal(r, denom[:, 2 * s:2 * s + 2]))
                own(vx.scalar_tensor_tensor(r[:, 1:2], denom[:, 2 * s:2 * s + 1], lam[:, 2:3], r[:, 1:2],
                                            ALU.mult, ALU.mult))
                vx.scalar_tensor_tensor(pr2[:, s, 0, 0:n], pr2[:, s, 1, 0:n], r[:, 1:2],
                                        pr2[:, s, 0, 0:n], ALU.mult, ALU.add).then_inc(p_ready, 1)

            biased(0)
            for i in range(n1):
                if i + 1 < n1:
                    biased(i + 1)
                difference(i)
            ve.wait_ge(sub_root, 1)
            own(vx.reciprocal(sumsq, sumsq))
            for qt in range(TT):
                o = o_rows(qt).rearrange("p (a b) -> p a b", a=HEADS)
                r = sumsq.rearrange("p (a b) -> p b a", b=TT)[:, qt, :]
                ins = vx.tensor_tensor(o, o, r.unsqueeze(2).broadcast_to([P, HEADS, P]), ALU.mult)
            ins.then_inc(sub_scaled, 1)
            split_x_lo(ve, "at_out", at_out)
            for j in range(4):
                ahead("w_o", j)
                computed(ve, "w_o", j)
                ins = vx.scalar_tensor_tensor(pre[:, 2 * j:2 * j + 2, :], h[:, 2 * j:2 * j + 2, :], ALPHA,
                                              pair(unit_bank(U0["w_o"] + j)[:, :]), ALU.mult, ALU.add)
                if j < 3:
                    free(ins, U0["w_o"] + j)
            ins.then_inc(stat_in, 1)
            layer_norm("mix1")
            experts(1)
            layer_norm("ffn1")


def columns(w):
    k, n = w.shape
    c = w.reshape(k // P, P, n // P, P).transpose(2, 1, 0, 3).reshape(n // P, P, k)
    if k == HW_:
        return c
    full = np.zeros((c.shape[0], P, HW_), np.float32)
    full[:, :, 0:k] = c
    return full


def wide_columns(w):
    return w.reshape(2, 4, P, -1, T).transpose(3, 0, 2, 1, 4).reshape(-1, P, HW_)


def rows_of(w):
    return w.reshape(-1, P, D)


def stream(a):
    win = columns(a["w_in"][0])
    v0 = 48 * P
    parts = [win[8:24], win[0:8], win[24:48], wide_columns(a["w_in"][0][:, v0:v0 + 12 * P]),
                       win[60:76], columns(a["w_conv_out"][0]),
                       columns(a["w_attn_out"][0]), columns(a["w_out"][0]),
                       columns(a["peer_w_query"][0]), columns(a["peer_down"][0].T),
                       rows_of(a["peer_up"][0])]
    pw1 = a["a_w_pw1_2"][0].reshape(D, 2, DT, P).transpose(0, 2, 1, 3).reshape(D, 2 * D)
    parts += [columns(pw1), columns(a["a_w_pw2_2"][0])]

    def moe(layer):
        def up_(name, e):
            return a[name][layer, e].reshape(4, 2, P, FE).transpose(0, 2, 1, 3).reshape(4, P, HW_)

        def down_(e):
            return rows_of(a["moe_w_down_2"][layer, e])

        gap = np.zeros((4, P, HW_), np.float32)
        out = []
        for e in range(NE):
            gate, up = up_("moe_w_gate_2", e), up_("moe_w_up_2", e)
            if e % EPG == 0:
                out += [gate, down_(e - 1) if e else gap, up]
            else:
                out += [gate, up, down_(e - 1)]
        out += [gap, down_(NE - 1)]
        return out

    w_kv = a["w_kv_2"]
    parts += moe(0) + [columns(w_kv[:, 0:D]), wide_columns(w_kv[:, D:]), columns(a["b_w_q_2"][0]), columns(a["b_w_o_2"][0])] + moe(1)
    out = np.concatenate(parts)
    return out


def vectors(a):
    names = [a["norm_mix"], a["conv_w"], a["gate_bias"], a["norm_ffn"], a["final_norm"],
             a["a_b_pw1_2"], a["a_w_dw_2"], a["a_b_dw_2"], a["a_ln_g_2"], a["a_ln_b_2"],
             a["a_b_pw2_2"], a["ln_mix_g_2"], a["ln_mix_b_2"], a["ln_ffn_g_2"], a["ln_ffn_b_2"],
             a["b_subln_g_2"]]
    return np.ascontiguousarray(np.concatenate([v.reshape(-1, P) for v in names]).T)


def kernel(**inputs):
    import concourse.bacc as bacc
    from concourse.bass_utils import run_bass_kernel_spmd

    a = {k: np.asarray(v) for k, v in inputs.items()}
    c = constants()
    arrays = {
        "x": np.ascontiguousarray(a["x"][0].T.reshape(DT, P, T).transpose(1, 0, 2)),
        "weights": stream(a), "vectors": vectors(a), "consts": c["consts"], "mask": c["mask"],
        "onehot": c["onehot"], "slots": c["slots"], "positions": a["positions"].reshape(T),
        "keys": np.ascontiguousarray(a["peer_sub_keys"][0].reshape(2 * PH, NK, P).transpose(2, 0, 1)),
        "router": np.ascontiguousarray(a["router_w_2"].reshape(DT, P, NE).transpose(1, 0, 2)),
        "rbias": a["router_bias_2"], "lam": a["b_lambda_2"].reshape(-1), "rel": a["rel_bias_2"],
    }
    nc = bacc.Bacc("TRN2", target_bir_lowering=False, num_devices=1)
    args = [nc.dram_tensor(f"in_{n}", v.shape, mybir.dt.from_np(v.dtype), kind="ExternalInput").ap()
            for n, v in arrays.items()]
    rows = nc.dram_tensor("bias_rows", (HEADS, P, RELS), F32, kind="Internal").ap()
    out = nc.dram_tensor("out", (P, DT, T), F32, kind="ExternalOutput").ap()
    build(nc, *args, rows, out)
    r = run_bass_kernel_spmd(nc, [{f"in_{n}": v for n, v in arrays.items()}], core_ids=[0])
    got = r.results[0]["out"]
    return got.transpose(1, 0, 2).reshape(D, T).T.reshape(1, T, D)
```
